# Optimizing a Trainium2 kernel written in Bass

```python
import math
import jax, jax.numpy as jnp
from jax import lax
import numpy as np

D_MODEL = 1024
BATCH = 1
SEQ = 2048
DEPTH = 1
DEC_BATCH = 8
DEC_SEQ = 16
PAST_LEN = 1024

CHUNK = 64
N_META = 16
Q_BLOCK = 128
H_A = 8
DH_A = 64
H_I = 4
D_IDX = 64
TOPK_MAX = 256
H_B = 4
DH_B = 64
DV_B = 2 * DH_B
D_MIX = H_A * DH_A + H_B * DV_B
D_FF = 4 * D_MODEL
SPLITS = (H_A * DH_A, DH_A, DH_A, H_I * D_IDX, D_IDX, H_I, H_B * 2 * DH_B, H_B * 2 * DH_B, H_B * DV_B)
D_IN = H_A * DH_A + 2 * DH_A + H_I * D_IDX + D_IDX + H_I + 2 * H_B * 2 * DH_B + H_B * DV_B
EPS = 1e-6

kernel_name = "hybrid_dsa_diffattn_streaming_step"

def _alibi_slopes(n):
    return jnp.asarray([2.0 ** (-8.0 * (i + 1) / n) for i in range(n)], jnp.float32)

def _rmsnorm(x, g):
    x32 = x.astype(jnp.float32)
    y = x32 * lax.rsqrt(jnp.mean(x32 * x32, axis=-1, keepdims=True) + EPS)
    return (y * g.astype(jnp.float32)).astype(x.dtype)

def _layernorm(x, g, b):
    x32 = x.astype(jnp.float32)
    mu = jnp.mean(x32, axis=-1, keepdims=True)
    xc = x32 - mu
    y = xc * lax.rsqrt(jnp.mean(xc * xc, axis=-1, keepdims=True) + EPS)
    return (y * g.astype(jnp.float32) + b.astype(jnp.float32)).astype(x.dtype)

def _project(h, g, w_in, kn_g, kn_b):
    B, T, _ = h.shape
    z = _rmsnorm(h, g) @ w_in
    cuts = [int(c) for c in np.cumsum(SPLITS)[:-1]]
    qa, ka, va, qi, ki, wi, qb, kb, vb = jnp.split(z, cuts, axis=-1)
    qa = qa.reshape(B, T, H_A, DH_A)
    qi = qi.reshape(B, T, H_I, D_IDX)
    ki = _layernorm(ki, kn_g, kn_b)
    qb = qb.reshape(B, T, H_B, 2, DH_B)
    kb = kb.reshape(B, T, H_B, 2, DH_B)
    vb = vb.reshape(B, T, H_B, DV_B)
    return qa, ka, va, qi, ki, wi, qb, kb, vb

def _dsa_attend(qa, qi, wi, qpos, qchunk, ka, va, ki, kpos, kchunk, k_top):
    f32 = jnp.float32
    rel = jax.nn.relu(jnp.einsum('bqhd,bld->bqhl', qi, ki).astype(f32) * (D_IDX ** -0.5))
    score = jnp.einsum('bqhl,bqh->bql', rel, wi.astype(f32) * (H_I ** -0.5))
    adm = kchunk[None, :] <= qchunk[:, None]
    score = jnp.where(adm[None], score, -jnp.inf)
    _, sel = lax.top_k(score, k_top)
    gather = jax.vmap(lambda t, i: t[i])
    k_sel = gather(ka, sel)
    v_sel = gather(va, sel)
    valid = jnp.take_along_axis(jnp.broadcast_to(adm[None], score.shape), sel, axis=-1)
    dist = jnp.abs(qpos[None, :, None] - kpos[sel]).astype(f32)
    logits = jnp.einsum('bqhd,bqkd->bqhk', qa, k_sel).astype(f32) * (DH_A ** -0.5)
    logits = logits - _alibi_slopes(H_A)[None, None, :, None] * dist[:, :, None, :]
    logits = jnp.where(valid[:, :, None, :], logits, -jnp.inf)
    p = jax.nn.softmax(logits, axis=-1).astype(va.dtype)
    return jnp.einsum('bqhk,bqkd->bqhd', p, v_sel)

def _diff_attend(qb, qpos, qchunk, kb, vb, kpos, kchunk, lam):
    f32 = jnp.float32
    logits = jnp.einsum('bqhcd,blhcd->bhcql', qb, kb).astype(f32) * (DH_B ** -0.5)
    dist = jnp.abs(qpos[:, None] - kpos[None, :]).astype(f32)
    logits = logits - _alibi_slopes(H_B)[None, :, None, None, None] * dist
    adm = kchunk[None, :] <= qchunk[:, None]
    logits = jnp.where(adm, logits, -jnp.inf)
    p = jax.nn.softmax(logits, axis=-1)
    a = (p[:, :, 0] - lam * p[:, :, 1]).astype(vb.dtype)
    return jnp.einsum('bhql,blhe->bqhe', a, vb)

def _blocked(fn, q_args, qpos, qchunk):
    n = qpos.shape[0]
    nb = -(-n // Q_BLOCK)
    pad = nb * Q_BLOCK - n

    def prep(a):
        a = jnp.pad(a, [(0, 0), (0, pad)] + [(0, 0)] * (a.ndim - 2))
        a = a.reshape((a.shape[0], nb, Q_BLOCK) + a.shape[2:])
        return jnp.moveaxis(a, 1, 0)

    posb = jnp.pad(qpos, (0, pad), mode='edge').reshape(nb, Q_BLOCK)
    chb = jnp.pad(qchunk, (0, pad), mode='edge').reshape(nb, Q_BLOCK)
    qs = tuple(prep(a) for a in q_args)
    out = lax.map(lambda xs: fn(*xs[0], xs[1], xs[2]), (qs, posb, chb))
    out = jnp.moveaxis(out, 0, 1)
    out = out.reshape((out.shape[0], nb * Q_BLOCK) + out.shape[3:])
    return out[:, :n]

def _finish(h, o_a, o_b, subln_g, lam_init, w_o, g_mlp, w_up, w_down):
    B, T, _ = h.shape
    o_b = _rmsnorm(o_b, subln_g) * (1.0 - lam_init)
    o = jnp.concatenate([o_a.reshape(B, T, H_A * DH_A), o_b.reshape(B, T, H_B * DV_B)], axis=-1)
    h = h + o @ w_o
    u = jax.nn.relu(_rmsnorm(h, g_mlp) @ w_up)
    return h + (u * u) @ w_down

def setup_inputs(seed: int = 0) -> dict:
    key = jax.random.key(seed)
    ks = jax.random.split(key, 24)
    f32 = jnp.float32
    nrm = lambda k, s, sc: jax.random.normal(k, s, f32) * sc
    return {
        'x_prompt': nrm(ks[0], (BATCH, SEQ, D_MODEL), 1.0),
        'x_sample': nrm(ks[1], (DEC_BATCH, DEC_SEQ, D_MODEL), 1.0),
        'cache_a_k': nrm(ks[2], (DEPTH, DEC_BATCH, PAST_LEN, DH_A), 1.0),
        'cache_a_v': nrm(ks[3], (DEPTH, DEC_BATCH, PAST_LEN, DH_A), 1.0),
        'cache_a_idx_k': nrm(ks[4], (DEPTH, DEC_BATCH, PAST_LEN, D_IDX), 1.0),
        'cache_b_k': nrm(ks[5], (DEPTH, DEC_BATCH, PAST_LEN, H_B, 2, DH_B), 1.0),
        'cache_b_v': nrm(ks[6], (DEPTH, DEC_BATCH, PAST_LEN, H_B, DV_B), 1.0),
        'meta_tokens': nrm(ks[7], (N_META, D_MODEL), 1.0),
        'attn_norm_g': 1.0 + nrm(ks[8], (DEPTH, D_MODEL), 0.02),
        'w_in': nrm(ks[9], (DEPTH, D_MODEL, D_IN), D_MODEL ** -0.5),
        'idx_k_norm_g': 1.0 + nrm(ks[10], (DEPTH, D_IDX), 0.02),
        'idx_k_norm_b': nrm(ks[11], (DEPTH, D_IDX), 0.02),
        'lambda_q1': nrm(ks[12], (DEPTH, DH_B), 0.1),
        'lambda_k1': nrm(ks[13], (DEPTH, DH_B), 0.1),
        'lambda_q2': nrm(ks[14], (DEPTH, DH_B), 0.1),
        'lambda_k2': nrm(ks[15], (DEPTH, DH_B), 0.1),
        'subln_g': 1.0 + nrm(ks[16], (DEPTH, DV_B), 0.02),
        'w_o': nrm(ks[17], (DEPTH, D_MIX, D_MODEL), D_MIX ** -0.5),
        'mlp_norm_g': 1.0 + nrm(ks[18], (DEPTH, D_MODEL), 0.02),
        'w_up': nrm(ks[19], (DEPTH, D_MODEL, D_FF), D_MODEL ** -0.5),
        'w_down': nrm(ks[20], (DEPTH, D_FF, D_MODEL), D_FF ** -0.5),
        'final_norm_g': 1.0 + nrm(ks[21], (D_MODEL,), 0.02),
    }

def reference(x_prompt, x_sample, cache_a_k, cache_a_v, cache_a_idx_k, cache_b_k, cache_b_v,
              meta_tokens, attn_norm_g, w_in, idx_k_norm_g, idx_k_norm_b,
              lambda_q1, lambda_k1, lambda_q2, lambda_k2, subln_g, w_o,
              mlp_norm_g, w_up, w_down, final_norm_g):
    f32 = jnp.float32
    B, S, _ = x_prompt.shape
    n = N_META + S
    meta = jnp.broadcast_to(meta_tokens[None].astype(x_prompt.dtype), (B, N_META, D_MODEL))
    h_p = jnp.concatenate([meta, x_prompt], axis=1)
    pos_p = jnp.arange(n, dtype=jnp.int32)
    chunk_p = jnp.where(pos_p < N_META, -1, (pos_p - N_META) // CHUNK)
    k_top_p = min(TOPK_MAX, S // 4)
    Ts = x_sample.shape[1]
    past = cache_a_k.shape[2]
    L = past + Ts
    pos_s = jnp.arange(L, dtype=jnp.int32)
    chunk_s = pos_s // CHUNK
    qpos_s = pos_s[past:]
    qchunk_s = chunk_s[past:]
    k_top_s = min(TOPK_MAX, L // 4)
    h_s = x_sample

    pak, pav, paik, pbk, pbv = [], [], [], [], []
    sak, sav, saik, sbk, sbv = [], [], [], [], []
    for l in range(DEPTH):
        lam_init = 0.8 - 0.6 * math.exp(-0.3 * l)
        lam = (jnp.exp(jnp.sum(lambda_q1[l].astype(f32) * lambda_k1[l].astype(f32)))
               - jnp.exp(jnp.sum(lambda_q2[l].astype(f32) * lambda_k2[l].astype(f32))) + lam_init)

        qa, ka, va, qi, ki, wi, qb, kb, vb = _project(h_p, attn_norm_g[l], w_in[l], idx_k_norm_g[l], idx_k_norm_b[l])
        o_a = _blocked(lambda a, b, c, p, cc: _dsa_attend(a, b, c, p, cc, ka, va, ki, pos_p, chunk_p, k_top_p),
                       (qa, qi, wi), pos_p, chunk_p)
        o_b = _blocked(lambda a, p, cc: _diff_attend(a, p, cc, kb, vb, pos_p, chunk_p, lam),
                       (qb,), pos_p, chunk_p)
        h_p = _finish(h_p, o_a, o_b, subln_g[l], lam_init, w_o[l], mlp_norm_g[l], w_up[l], w_down[l])
        pak.append(ka); pav.append(va); paik.append(ki); pbk.append(kb); pbv.append(vb)

        qa, ka_n, va_n, qi, ki_n, wi, qb, kb_n, vb_n = _project(h_s, attn_norm_g[l], w_in[l], idx_k_norm_g[l], idx_k_norm_b[l])
        ka_all = jnp.concatenate([cache_a_k[l].astype(ka_n.dtype), ka_n], axis=1)
        va_all = jnp.concatenate([cache_a_v[l].astype(va_n.dtype), va_n], axis=1)
        ki_all = jnp.concatenate([cache_a_idx_k[l].astype(ki_n.dtype), ki_n], axis=1)
        kb_all = jnp.concatenate([cache_b_k[l].astype(kb_n.dtype), kb_n], axis=1)
        vb_all = jnp.concatenate([cache_b_v[l].astype(vb_n.dtype), vb_n], axis=1)
        o_a = _dsa_attend(qa, qi, wi, qpos_s, qchunk_s, ka_all, va_all, ki_all, pos_s, chunk_s, k_top_s)
        o_b = _diff_attend(qb, qpos_s, qchunk_s, kb_all, vb_all, pos_s, chunk_s, lam)
        h_s = _finish(h_s, o_a, o_b, subln_g[l], lam_init, w_o[l], mlp_norm_g[l], w_up[l], w_down[l])
        sak.append(ka_n); sav.append(va_n); saik.append(ki_n); sbk.append(kb_n); sbv.append(vb_n)

    y_prompt = _rmsnorm(h_p[:, N_META:], final_norm_g)
    y_sample = _rmsnorm(h_s, final_norm_g)
    return (y_prompt, y_sample,
            jnp.stack(pak), jnp.stack(pav), jnp.stack(paik), jnp.stack(pbk), jnp.stack(pbv),
            jnp.stack(sak), jnp.stack(sav), jnp.stack(saik), jnp.stack(sbk), jnp.stack(sbv))


_drawn_inputs = setup_inputs


def setup_inputs(seed=0):
    import zlib

    import numpy as np

    out = dict(_drawn_inputs(seed))
    spreads = {}
    factors = {'lambda_q2': 8.0,
     'subln_g': 5.308,
     'mlp_norm_g': 3.489,
     'final_norm_g': 7.623,
     'idx_k_norm_b': 2.766}
    for name, (base, spread) in spreads.items():
        noise = np.random.default_rng([zlib.crc32(name.encode()), seed]).standard_normal(out[name].shape)
        drawn = base * np.exp(spread * noise) if base else spread * noise
        out[name] = __import__('jax').numpy.asarray(drawn.astype(out[name].dtype))
    for name, factor in factors.items():
        out[name] = (out[name] * factor).astype(out[name].dtype)
    return out
```

```python
from contextlib import ExitStack

import numpy as np
import concourse.bass as bass
from concourse import mybir

F32 = mybir.dt.float32
F32R = mybir.dt.float32r
BF16 = mybir.dt.bfloat16
ALU = mybir.AluOpType
ACT = mybir.ActivationFunctionType
AX = mybir.AxisListType
ds = bass.ds

P = 128
D_MODEL, D_FF = 1024, 4096
N_META, SEQ, CHUNK = 16, 2048, 64
DEC_BATCH, DEC_SEQ, PAST = 8, 16, 1024
TOPK = 256
H_A, H_I, H_B, DH, DV_B = 8, 4, 4, 64, 128
EPS = 1e-6
LAM_INIT = 0.2

PT = SEQ // P
NT = PT + 1
ROWS = N_META + NT * P
PKEYS = N_META + SEQ
SKEYS = PAST + DEC_SEQ
DC = D_MODEL // P
KM = 2 + 2 * H_B
QM = H_A + H_I + 2 * H_B
KCOLS = KM * DH
VCOLS = DH + H_B * DV_B
KV = KCOLS + VCOLS
QCOLS = QM * DH
QW = QCOLS + H_I
BIG = float(2 ** 100)

SLOPE_A = [2.0 ** -(h + 1) for h in range(H_A)]
SLOPE_B = [2.0 ** (-2 * (h + 1)) for h in range(H_B)]


def banks_of(cols):
    return [(a, min(512, cols - a)) for a in range(0, cols, 512)]


def free_semaphores(nc, sems):
    nc.clear_and_free_semaphores(sems)
    nc.all_engine_barrier()


def project(nc, keys, xT, x, w, gain, ident, row_tab, kn_gb, z_out, t_out, wi_out):
    cols = KV if keys else QW
    maps = KM if keys else QM
    banks = banks_of(cols)
    NB = len(banks)
    parts = 1 if keys else 2
    blocks = maps * parts
    tgroups = [(g, min(4, blocks - g)) for g in range(0, blocks, 4)]
    NG = len(tgroups)
    TB = min(8 - NB, NG)
    tag = "k" if keys else "q"

    sems = []
    with ExitStack() as ctx:
        def sb(name, shape, dt=F32):
            return ctx.enter_context(nc.sbuf_tensor(tag + name, shape, dt))

        def sem(name):
            sems.append(nc.alloc_semaphore(tag + name))
            return sems[-1]

        w_hi = sb("w_hi", [P, DC, cols], F32R)
        w_lo = sb("w_lo", [P, DC, cols], F32R)
        w_raw = [sb(f"w_raw{i}", [P, cols]) for i in range(2)]
        gain_sb = sb("gain", [P, DC])
        xT_raw = [sb(f"xT_raw{i}", [P, DC, P]) for i in range(2)]
        x_hi = [sb(f"x_hi{i}", [P, DC, P], F32R) for i in range(2)]
        x_lo = [sb(f"x_lo{i}", [P, DC, P], F32R) for i in range(2)]
        x_row = [sb(f"x_row{i}", [P, D_MODEL]) for i in range(2)]
        square = sb("square", [P, D_MODEL])
        ss = sb("ss", [P, 2])
        rms = sb("rms", [P, 2])
        const = sb("const", [P, 3])
        z = sb("z", [P, cols])
        scale_tab = sb("scale", [P, cols]) if not keys else None
        if keys:
            stack = sb("stack", [P, KM, 2, DH], F32R)
            ln = sb("ln", [P, 2, DH])
            st = sb("st", [P, 4])
            lnw = sb("lnw", [P, DH])
            kn = sb("kn", [P, 2, DH])
        else:
            stack = sb("stack", [P, QM, 2, 2, DH], F32R)
        tz = sb("tz", [P, blocks, P])
        idn = sb("idn", [P, P])
        acc = [ctx.enter_context(nc.psum_tensor(f"{tag}acc{b}", [P, 512], F32)) for b in range(NB)]
        tps = [ctx.enter_context(nc.psum_tensor(f"{tag}tps{b}", [P, 4, P], F32)) for b in range(TB)]

        s_const = sem("s_const")
        s_const2 = sem("s_const2")
        s_wraw = [sem(f"s_wraw{i}") for i in range(2)]
        s_whi = sem("s_whi")
        s_wlo = sem("s_wlo")
        s_x = [sem(f"s_x{i}") for i in range(2)]
        s_xhi = sem("s_xhi")
        s_xlo = sem("s_xlo")
        s_ss = sem("s_ss")
        s_eps = sem("s_eps")
        s_rms = sem("s_rms")
        s_acc = sem("s_acc")
        s_z = sem("s_z")
        s_ln = sem("s_ln")
        s_var = sem("s_var")
        s_istd = sem("s_istd")
        s_shi = sem("s_shi")
        s_slo = sem("s_slo")
        s_zst = sem("s_zst")
        s_tr = sem("s_tr")
        s_tz = sem("s_tz")
        s_tst = sem("s_tst")
        LN = 5

        last = NT if keys else NT - 1
        PAIRS = (16 - 2) // 2

        def rows_of(n):
            return N_META if keys and isinstance(n, int) and n == 0 else P

        def row_of(n):
            if keys:
                return 0 if isinstance(n, int) and n == 0 else n * P + (N_META - P)
            return n * P + N_META

        def run(engine, step):
            for n in (0, 1):
                step(n, n % 2, n // 2)
            with engine.Fori(0, PAIRS, 1) as j:
                step(j * 2 + 2, 0, j + 1)
                step(j * 2 + 3, 1, j + 1)
            for n in range(16, last + 1):
                step(n, n % 2, n // 2)

        def after(n, k):
            return not isinstance(n, int) or n >= k

        block = ctx.enter_context(nc.Block())

        @block.sync
        def _(sp):
            sp.dma_start(gain_sb[:, :], gain).then_inc(s_const, 16)
            sp.dma_start(idn[:, :], ident).then_inc(s_const, 16)
            if keys:
                sp.dma_start(kn[:, :, :], kn_gb).then_inc(s_const, 16)
            else:
                sp.dma_start(scale_tab[:, :], row_tab).then_inc(s_const, 16)

            def load(n, par, m):
                if after(n, 2):
                    sp.wait_ge(s_xlo, n - 1)
                    sp.wait_ge(s_ss, n - 1)
                rows, row = rows_of(n), row_of(n)
                sp.dma_start(xT_raw[par][:, :, 0:rows], xT[:, :, ds(row, rows)]).then_inc(s_x[par], 16)
                sp.dma_start(x_row[par][0:rows, :], x[ds(row, rows), :]).then_inc(s_x[par], 16)

            load(0, 0, 0)
            for c in range(DC):
                if c >= 2:
                    sp.wait_ge(s_wlo, c - 1)
                sp.dma_start(w_raw[c % 2][:, :], w[:, c, :]).then_inc(s_wraw[c % 2], 16)

            def step(n, par, m):
                if not (isinstance(n, int) and n == last):
                    load(n + 1, 1 - par, m + par)
                if keys:
                    sp.wait_ge(s_ln, n * LN + LN)
                    sp.dma_start(z_out[ds(row_of(n), rows_of(n)), :], z[0:rows_of(n), :]).then_inc(s_zst, 16)
                else:
                    sp.wait_ge(s_z, n * NB + NB)
                    sp.dma_start(wi_out[ds(n * P, P), :], z[:, QCOLS:QW]).then_inc(s_zst, 16)
            run(sp, step)
            sp.wait_ge(s_zst, 16 * (last + 1))

        @block.gpsimd
        def _(pool):
            for i, value in enumerate((1.0 / D_MODEL, EPS, -0.5)):
                pool.memset(const[:, i:i + 1], value).then_inc(s_const2, 1)
            pool.wait_ge(s_const2, 3)

            def inverse_rms(n, par):
                rows = rows_of(n)
                if after(n, 2):
                    pool.wait_ge(s_z, n * NB - NB)
                pool.wait_ge(s_ss, n + 1)
                v = rms[0:rows, par:par + 1]
                pool.tensor_tensor(v, ss[0:rows, par:par + 1], const[0:rows, 0:1], ALU.mult).then_inc(s_eps, 1)
                pool.wait_ge(s_eps, n * 2 + 1)
                pool.tensor_tensor(v, v, const[0:rows, 1:2], ALU.add).then_inc(s_eps, 1)
                pool.wait_ge(s_eps, n * 2 + 2)
                pool.tensor_tensor(v, v, const[0:rows, 2:3], ALU.pow).then_inc(s_rms, 1)

            inverse_rms(0, 0)

            def step(n, par, m):
                if not (isinstance(n, int) and n == last):
                    inverse_rms(n + 1, 1 - par)
                if keys:
                    rows = rows_of(n)
                    pool.wait_ge(s_var, n + 1)
                    pool.tensor_tensor(st[0:rows, 3:4], st[0:rows, 2:3], const[0:rows, 2:3],
                                       ALU.pow).then_inc(s_istd, 1)
            run(pool, step)

        @block.tensor
        def _(pe):
            pe.wait_ge(s_const, 48)
            flat = stack[:, :, :, :].rearrange("p a b c -> p (a b c)") if keys else \
                stack[:, :, :, :, :].rearrange("p a b c e -> p (a b c e)")

            def products(n, par, b):
                a, size = banks[b]
                rows = rows_of(n)
                if after(n, 1):
                    pe.wait_ge(s_z, n * NB + (b + 1 - NB))
                for c in range(DC):
                    if isinstance(n, int) and n == 0 and b == 0:
                        pe.wait_ge(s_wlo, c + 1)
                    for k, (xs, ws) in enumerate(((x_hi, w_hi), (x_hi, w_lo), (x_lo, w_hi))):
                        mm = pe.matmul(acc[b][0:rows, 0:size], xs[par][:, c, 0:rows], ws[:, c, a:a + size],
                                       start=(c == 0 and k == 0), stop=(c == DC - 1 and k == 2))
                mm.then_inc(s_acc, 1)

            def transposes(n):
                rows = rows_of(n)
                pe.wait_ge(s_slo, n + 1)
                for k, (g, size) in enumerate(tgroups):
                    if k >= TB or after(n, 1):
                        pe.wait_ge(s_tz, n * NG + (k + 1 - TB))
                    for q in range(size):
                        tr = pe.transpose(tps[k % TB][:, q, 0:rows],
                                          flat[0:rows, (g + q) * P:(g + q + 1) * P].bitcast(F32),
                                          idn[0:rows, 0:rows])
                    tr.then_inc(s_tr, 1)

            def step(n, par, m):
                pe.wait_ge(s_xlo, n + 1)
                products(n, par, 0)
                products(n, par, 1)
                if after(n, 1):
                    transposes(n - 1)
                products(n, par, 2)
            run(pe, step)
            transposes(last)

        @block.scalar
        def _(act):
            act.wait_ge(s_const, 48)

            def x_parts(n, par, m):
                rows = rows_of(n)
                act.wait_ge(s_x[par], m * 32 + 32)
                if after(n, 2):
                    act.wait_ge(s_acc, n * NB - NB)
                act.activation(x_hi[par][:, :, 0:rows], xT_raw[par][:, :, 0:rows],
                               ACT.Copy).then_inc(s_xhi, 1)
                if after(n, 1):
                    act.wait_ge(s_ss, n)
                if after(n, 2):
                    act.wait_ge(s_rms, n - 1)
                act.activation(square[0:rows, :], x_row[par][0:rows, :], ACT.Square,
                               accum_out=ss[0:rows, par:par + 1]).then_inc(s_ss, 1)

            def take(n, tile):
                rows = rows_of(n)
                if after(n, 1):
                    act.wait_ge(s_tst, n * 16)
                for k, (g, size) in enumerate(tgroups):
                    act.wait_ge(s_tr, n * NG + (k + 1))
                    act.activation(tz[:, g:g + size, 0:rows], tps[k % TB][:, 0:size, 0:rows],
                                   ACT.Copy).then_inc(s_tz, 1)
                act.wait_ge(s_tz, n * NG + NG)
                if keys:
                    dst = t_out[:, :, ds(row_of(n), rows)]
                else:
                    dst = t_out[ds(n * P, P), :].rearrange("p (b q) -> p b q", b=blocks)
                act.dma_start(dst, tz[:, :, 0:rows]).then_inc(s_tst, 16)

            x_parts(0, 0, 0)
            for c in range(DC):
                act.wait_ge(s_wraw[c % 2], 16 * (c // 2 + 1))
                act.activation(w_hi[:, c, :], w_raw[c % 2][:, :], ACT.Copy,
                               scale=gain_sb[:, c:c + 1]).then_inc(s_whi, 1)

            def step(n, par, m):
                if not (isinstance(n, int) and n == last):
                    x_parts(n + 1, 1 - par, m + par)
                if after(n, 1):
                    take(n - 1, None)
            run(act, step)
            take(last, None)
            act.wait_ge(s_tst, 16 * (last + 1))

        @block.vector
        def _(dve):
            dve.wait_ge(s_const, 48)

            def split_x(n, par):
                rows = rows_of(n)
                dve.wait_ge(s_xhi, n + 1)
                dve.tensor_tensor(x_lo[par][:, :, 0:rows], xT_raw[par][:, :, 0:rows],
                                  x_hi[par][:, :, 0:rows].bitcast(F32), ALU.subtract).then_inc(s_xlo, 1)

            split_x(0, 0)
            for c in range(DC):
                dve.wait_ge(s_whi, c + 1)
                dve.scalar_tensor_tensor(w_lo[:, c, :], w_raw[c % 2][:, :], gain_sb[:, c:c + 1],
                                         w_hi[:, c, :].bitcast(F32), ALU.mult, ALU.subtract).then_inc(s_wlo, 1)

            def take(n, par, b):
                rows = rows_of(n)
                a, size = banks[b]
                if b == 0:
                    dve.wait_ge(s_rms, n + 1)
                    if after(n, 1):
                        dve.wait_ge(s_zst, n * 16)
                        dve.wait_ge(s_slo, n)
                dve.wait_ge(s_acc, n * NB + (b + 1))
                if keys:
                    dve.tensor_scalar(z[0:rows, a:a + size], acc[b][0:rows, 0:size],
                                      rms[0:rows, par:par + 1], None, ALU.mult).then_inc(s_z, 1)
                else:
                    dve.scalar_tensor_tensor(z[0:rows, a:a + size], acc[b][0:rows, 0:size],
                                             rms[0:rows, par:par + 1], scale_tab[0:rows, a:a + size],
                                             ALU.mult, ALU.mult).then_inc(s_z, 1)

            def layer_norm(n):
                rows = rows_of(n)
                ki = z[0:rows, DH:2 * DH]
                dve.tensor_reduce(st[0:rows, 0:1], ki, AX.X, ALU.add).then_inc(s_ln, 1)
                dve.wait_ge(s_ln, n * LN + 1)
                dve.tensor_scalar(st[0:rows, 1:2], st[0:rows, 0:1], 1.0 / DH, None, ALU.mult).then_inc(s_ln, 1)
                dve.wait_ge(s_ln, n * LN + 2)
                dve.tensor_scalar(ln[0:rows, 0, :], ki, st[0:rows, 1:2], None, ALU.subtract).then_inc(s_ln, 1)
                dve.wait_ge(s_ln, n * LN + 3)
                dve.tensor_tensor_reduce(out=lnw[0:rows, :], in0=ln[0:rows, 0, :], in1=ln[0:rows, 0, :],
                                         scale=1.0 / DH, scalar=EPS, op0=ALU.mult, op1=ALU.add,
                                         accum_out=st[0:rows, 2:3]).then_inc(s_var, 1)
                dve.wait_ge(s_istd, n + 1)
                dve.scalar_tensor_tensor(ln[0:rows, 1, :], ln[0:rows, 0, :], st[0:rows, 3:4],
                                         kn[0:rows, 0, :], ALU.mult, ALU.mult).then_inc(s_ln, 1)
                dve.wait_ge(s_ln, n * LN + 4)
                dve.tensor_tensor(ki, ln[0:rows, 1, :], kn[0:rows, 1, :], ALU.add).then_inc(s_ln, 1)
                dve.wait_ge(s_ln, n * LN + 5)

            def stacks(n):
                rows = rows_of(n)
                maps = z[0:rows, 0:blocks_cols].rearrange("p (m d) -> p m d", d=DH)
                if after(n, 1):
                    dve.wait_ge(s_tr, n * NG)
                if keys:
                    dve.tensor_copy(stack[0:rows, :, 0, :], maps).then_inc(s_shi, 1)
                    dve.wait_ge(s_shi, n + 1)
                    dve.tensor_tensor(stack[0:rows, :, 1, :], maps, stack[0:rows, :, 0, :].bitcast(F32),
                                      ALU.subtract).then_inc(s_slo, 1)
                else:
                    dve.tensor_copy(stack[0:rows, :, 0, 0, :], maps).then_inc(s_shi, 1)
                    dve.tensor_copy(stack[0:rows, :, 0, 1, :], maps)
                    dve.wait_ge(s_shi, n + 1)
                    dve.tensor_tensor(stack[0:rows, :, 1, 0, :], maps, stack[0:rows, :, 0, 0, :].bitcast(F32),
                                      ALU.subtract)
                    dve.tensor_tensor(stack[0:rows, :, 1, 1, :], maps, stack[0:rows, :, 0, 0, :].bitcast(F32),
                                      ALU.subtract).then_inc(s_slo, 1)

            blocks_cols = KCOLS if keys else QCOLS

            def step(n, par, m):
                take(n, par, 0)
                if not (isinstance(n, int) and n == last):
                    split_x(n + 1, 1 - par)
                take(n, par, 1)
                take(n, par, 2)
                dve.wait_ge(s_z, n * NB + NB)
                if keys:
                    layer_norm(n)
                stacks(n)
            run(dve, step)
    free_semaphores(nc, sems)



HALVINGS = 25
SEL_FIRST = 7
SEL_EACH = 3
SEL_LAST = 9
SEL = SEL_FIRST + HALVINGS * SEL_EACH + SEL_LAST


def count_step(h):
    return SEL_FIRST + h * SEL_EACH


def halving_widths(engine, powers, made):
    for h in range(HALVINGS):
        engine.memset(powers[:, h:h + 1], 2.0 ** (1 - h)).then_inc(made, 1)


def select_step(dve, s_sel, base, k, S, D, table, junk, v, powers, widths, n, inadmissible=None, by_sign=lambda h: False):
    lo, hi, mid, cnt, step, need, bound = (v[:, i:i + 1] for i in range(7))
    if k > 0:
        dve.wait_ge(s_sel, base + k)
    if k == 0:
        ins = dve.tensor_reduce(lo, S, AX.X, ALU.min)
    elif k == 1:
        if inadmissible is None:
            ins = dve.tensor_copy(mid, lo)
        else:
            ins = dve.memset(inadmissible, -BIG)
    elif k == 2:
        ins = dve.tensor_reduce(hi, S, AX.X, ALU.max)
    elif k == 3:
        ins = dve.tensor_scalar(bound, lo, -1.0, 1e-30, ALU.mult, ALU.max)
    elif k == 4:
        ins = dve.tensor_tensor(bound, bound, hi, ALU.max)
    elif k == 5:
        i32 = mybir.dt.int32
        ins = dve.tensor_scalar(bound.bitcast(i32), bound.bitcast(i32), 0x7F800000, None, ALU.bitwise_and)
    elif k == 6:
        ins = dve.tensor_scalar(widths, powers, bound, None, ALU.mult)
    elif k < SEL_FIRST + HALVINGS * SEL_EACH:
        h, q = divmod(k - SEL_FIRST, SEL_EACH)
        width = widths[:, h:h + 1]
        if q == 0:
            if h == 0:
                ins = dve.tensor_scalar(junk, S, 0.0, 0.0, ALU.is_ge, ALU.add, accum_out=cnt)
            else:
                ins = dve.tensor_scalar(junk, S, mid, 0.0, ALU.is_ge, ALU.add, accum_out=cnt)
        elif q == 1:
            enough = ALU.is_ge, TOPK - 0.5
            if by_sign(h):
                enough = ALU.is_le, n - 2 * TOPK + 0.5
            ins = dve.tensor_scalar(step, cnt, enough[1], 0.5 if h < HALVINGS - 1 else 1.0, enough[0], ALU.subtract)
        elif h == 0:
            ins = dve.tensor_scalar(mid, step, width, None, ALU.mult)
        else:
            ins = dve.scalar_tensor_tensor(mid if h < HALVINGS - 1 else lo, step, width, mid, ALU.mult, ALU.add)
    else:
        q = k - SEL_FIRST - HALVINGS * SEL_EACH
        if q == 0:
            ins = dve.tensor_tensor(hi, lo, widths[:, HALVINGS - 1:HALVINGS], ALU.add)
        elif q == 1:
            ins = dve.tensor_scalar(D, S, hi, 0.0, ALU.is_gt, ALU.add, accum_out=cnt)
        elif q == 2:
            ins = dve.tensor_scalar(need, cnt, -1.0, float(TOPK), ALU.mult, ALU.add)
        elif q == 3:
            ins = dve.scalar_tensor_tensor(D, S, lo, D, ALU.is_ge, ALU.subtract)
        elif q == 4:
            ins = dve.tensor_tensor_scan(D, D, D, 0.0, ALU.add, ALU.bypass)
        elif q == 5:
            ins = dve.tensor_scalar(D, D, need, None, ALU.is_gt)
        elif q == 6:
            ins = dve.scalar_tensor_tensor(D, S, lo, D, ALU.is_lt, ALU.max)
        elif q == 7:
            ins = dve.scalar_tensor_tensor(D, S, hi, D, ALU.is_le, ALU.mult)
        else:
            ins = dve.scalar_tensor_tensor(D, D, -BIG, table, ALU.mult, ALU.add)
    ins.then_inc(s_sel, 1)


def attend_prompt(nc, kT, kv, qT, wi, dist, ident, lambdas, sub_g, oT):
    JOBS = QM - H_I
    L = 1024
    n_of = [N_META + P * (t + 1) for t in range(PT)]
    blk = [t + 2 for t in range(PT)]
    halves = [-(-n // L) for n in n_of]
    groups = [-(-b // 4) for b in blk]
    XW = PKEYS + P - N_META
    NG = PT * JOBS

    sems = []
    with ExitStack() as ctx:
        def sb(name, shape, dt=F32):
            return ctx.enter_context(nc.sbuf_tensor("p" + name, shape, dt))

        def sem(name):
            sems.append(nc.alloc_semaphore("p" + name))
            return sems[-1]

        K = sb("K", [P, KM, PKEYS], F32R)
        V = sb("V", [P, PT + 1, VCOLS])
        QI = sb("QI", [P, H_I, 2, P], F32R)
        QA = sb("QA", [P, H_A, 2, P], F32R)
        QB = sb("QB", [P, 2 * H_B, 2, P], F32R)
        W = sb("W", [P, PT, H_I])
        S = sb("S", [P, PKEYS])
        DA = sb("DA", [P, PKEYS])
        DT = sb("DT", [P, PKEYS])
        X = [sb(f"X{i}", [P, XW]) for i in range(2)]
        junk = sb("junk", [P, PKEYS], mybir.dt.int8)
        PTr = [sb(f"PTr{i}", [P, 4, P]) for i in range(3)]
        O = [sb(f"O{i}", [P, D_MODEL]) for i in range(2)]
        OM = sb("OM", [P, DV_B])
        OT = sb("OT", [P, DC, P])
        R = [sb("R", [P, L]), OT[:, :, :].rearrange("p c q -> p (c q)")]
        gB = sb("gB", [P, DV_B])
        lam4 = sb("lam4", [P, 4, DH])
        lv = sb("lv", [P, 8])
        half = sb("half", [P, 4])
        sv = sb("sv", [P, 8])
        powers = sb("powers", [P, HALVINGS])
        widths = sb("widths", [P, HALVINGS])
        mx = sb("mx", [P, 2, 4])
        nm = sb("nm", [P, 2])
        sm = sb("sm", [P, 2])
        ri = sb("ri", [P, 2])
        rl = sb("rl", [P, 1])
        fs = sb("fs", [P, 8])
        idn = sb("idn", [P, P])
        LG = ctx.enter_context(nc.psum_tensor("pLG", [P, 2, L], F32))
        TP = [ctx.enter_context(nc.psum_tensor(f"pTP{i}", [P, 4, P], F32)) for i in range(2)]
        PV = [ctx.enter_context(nc.psum_tensor(f"pPV{i}", [P, 512], F32)) for i in range(2)]

        s_c = sem("s_c")
        s_k = [sem(f"s_k{t}") for t in range(PT)]
        s_v = [sem(f"s_v{t}") for t in range(4)]
        s_qi, s_qa, s_qb = sem("s_qi"), sem("s_qa"), sem("s_qb")
        s_x0 = sem("s_x0")
        s_lam = sem("s_lam")
        s_half = sem("s_half")
        s_il = sem("s_il")
        s_ir = sem("s_ir")
        s_ia = sem("s_ia")
        s_pow = sem("s_pow")
        s_sel = sem("s_sel")
        s_qk = sem("s_qk")
        s_lx = sem("s_lx")
        s_nm = sem("s_nm")
        s_ex = sem("s_ex")
        s_tr = sem("s_tr")
        s_pt = sem("s_pt")
        s_pvg = sem("s_pvg")
        s_ri = sem("s_ri")
        s_rl = sem("s_rl")
        s_out = sem("s_out")
        s_fq = sem("s_fq")
        s_fe = sem("s_fe")
        s_fr = sem("s_fr")
        s_fo = sem("s_fo")
        s_ft = sem("s_ft")
        s_fc = sem("s_fc")
        s_fs = sem("s_fs")

        def halves_before(g):
            return sum(halves[i // JOBS] for i in range(g))

        def groups_before(g):
            return sum(groups[i // JOBS] for i in range(g))

        def idx_before(t):
            return sum(H_I * halves[i] for i in range(1, t))

        def score_halves(t, m):
            return range(m * 2 * halves[t], (m + 1) * 2 * halves[t])

        def bank_users():
            logits, banks, use_of, bank_use = [], [], {}, {}

            def logit(kind, n, free):
                use_of[kind, n] = len(logits)
                logits.append(free)

            def bank(kind, n, free):
                bank_use[kind, n] = len(banks)
                banks.append(free)

            for g in range(-2, NG):
                if g >= 0 and g % JOBS < 2 and g // JOBS + 1 < PT:
                    t = g // JOBS + 1
                    for k in score_halves(t, g % JOBS):
                        logit("i", idx_before(t) + k, (s_ir, idx_before(t) + k + 1))
                if g + 2 < NG:
                    for k in range(halves[(g + 2) // JOBS]):
                        logit("q", halves_before(g + 2) + k, (s_lx, halves_before(g + 2) + k + 1))
                if g >= 0:
                    if g % JOBS == 2 and g >= JOBS:
                        for k in range(2 * (g // JOBS) - 2, 2 * (g // JOBS)):
                            bank("f", k, (s_fc, k + 1))
                    for k in range(groups[g // JOBS]):
                        bank("p", groups_before(g) + k, (s_pt, groups_before(g) + k + 1))
            for k in range(2 * PT - 2, 2 * PT):
                bank("f", k, (s_fc, k + 1))
            return logits, banks, use_of, bank_use
        logit_users, bank_of, use_of, bank_use = bank_users()

        def by_sign(h):
            return h % 2 == 0

        def counted_by_sign(m):
            return 2 * (m - 1) if 0 <= 2 * (m - 1) < HALVINGS else None

        def select_steps(m):
            last = count_step(HALVINGS)
            if m == 0:
                return (0, 0), (0, 0)
            if m == 1:
                return (0, 0), (0, SEL_FIRST)
            h = counted_by_sign(m - 1)
            if h is None:
                return (last + 6, SEL), (SEL, SEL)
            if h == HALVINGS - 1:
                return (count_step(h) + 1, last), (last, last + 6)
            return (count_step(h) + 1, count_step(h + 1)), (count_step(h + 1), count_step(h + 2))

        block = ctx.enter_context(nc.Block())

        @block.sync
        def _(sp):
            for dst, src in ((DT[:, :], dist), (idn[:, :], ident), (gB[:, :], sub_g),
                             (lam4[:, :, :], lambdas), (W[:, :, :], wi)):
                sp.dma_start(dst, src).then_inc(s_c, 16)

            def keys(t):
                a = n_of[t] - P if t else 0
                sp.dma_start(K[:, :, a:n_of[t]].bitcast(F32), kT[:, :, a:n_of[t]]).then_inc(s_k[t], 16)

            def queries(dst, t, m, maps, done):
                sp.dma_start(dst[:, :, :, :].bitcast(F32).rearrange("p m u q -> p (m u q)"),
                             qT[t * P:(t + 1) * P, m * 2 * P:(m + maps) * 2 * P]).then_inc(done, 16)

            def values(c):
                a, b = (4 * c, 4 * c + 4) if c < 3 else (12, PT + 1)
                sp.dma_start(V[:, a:b, :], kv[a * P:b * P, KCOLS:KV].rearrange("(b p) v -> p b v", p=P))\
                    .then_inc(s_v[c], 16)

            def store(t):
                sp.wait_ge(s_fc, 2 * t + 2)
                sp.dma_start(oT[:, :, t * P:(t + 1) * P], OT[:, :, :]).then_inc(s_fs, 16)

            keys(0)
            queries(QA, 0, 0, H_A, s_qa)
            queries(QB, 0, H_A + H_I, 2 * H_B, s_qb)
            queries(QI, 1, H_A, H_I, s_qi)
            values(0)
            keys(1)
            keys(2)
            for c in range(1, 4):
                values(c)
            for t in range(3, PT):
                keys(t)
            for t in range(PT):
                if 1 <= t and t + 1 < PT:
                    sp.wait_ge(s_il, idx_before(t + 1))
                    queries(QI, t + 1, H_A, H_I, s_qi)
                if t > 0:
                    store(t - 1)
                if t + 1 < PT:
                    sp.wait_ge(s_qk, halves_before(t * JOBS + H_A))
                    queries(QA, t + 1, 0, H_A, s_qa)
                    sp.wait_ge(s_qk, halves_before((t + 1) * JOBS))
                    queries(QB, t + 1, H_A + H_I, 2 * H_B, s_qb)
            store(PT - 1)
            sp.wait_ge(s_fs, 16 * PT)

        @block.gpsimd
        def _(pool):
            pool.memset(half[:, :], -0.5).then_inc(s_half, 1)
            halving_widths(pool, powers, s_pow)
            pool.wait_ge(s_half, 1)
            for t in range(PT):
                pool.wait_ge(s_fq, 4 * (t + 1))
                pool.tensor_scalar(fs[:, 4:8], fs[:, 0:4], 1.0 / DV_B, EPS, ALU.mult, ALU.add)\
                    .then_inc(s_fe, 1)
                pool.wait_ge(s_fe, t + 1)
                pool.tensor_tensor(fs[:, 4:8], fs[:, 4:8], half[:, :], ALU.pow).then_inc(s_fr, 1)

        @block.tensor
        def _(pe):
            pe.wait_ge(s_c, 80)
            used = {"logits": 0, "banks": 0}

            def free_half():
                u = used["logits"]
                if u >= 2:
                    pe.wait_ge(*logit_users[u - 2])
                used["logits"] += 1
                return LG[:, u % 2, :]

            def free_bank():
                u = used["banks"]
                if u >= 2:
                    pe.wait_ge(*bank_of[u - 2])
                used["banks"] += 1
                return TP[u % 2]

            def logits(t, q, km, signal):
                for a in range(0, n_of[t], L):
                    dst = free_half()
                    for b in range(a, min(a + L, n_of[t]), 512):
                        size = min(512, n_of[t] - b)
                        for u in range(2):
                            mm = pe.matmul(dst[:, b - a:b - a + size], q[:, u, :], K[:, km, b:b + size],
                                           start=(u == 0), stop=(u == 1))
                    mm.then_inc(signal, 1)

            def scores(t, m):
                if m == 0:
                    pe.wait_ge(s_qi, 16 * t)
                    pe.wait_ge(s_k[t], 16)
                for h in (2 * m, 2 * m + 1):
                    logits(t, QI[:, h], 1, s_il)

            def queries_keys(g):
                t, m = divmod(g, JOBS)
                if m == 0:
                    pe.wait_ge(s_k[t], 16)
                    pe.wait_ge(s_qa, 16 * (t + 1))
                if m < H_A:
                    logits(t, QA[:, m], 0, s_qk)
                else:
                    if m == H_A:
                        pe.wait_ge(s_qb, 16 * (t + 1))
                    logits(t, QB[:, m - H_A], 2 + m - H_A, s_qk)

            def apply(g):
                t, m = divmod(g, JOBS)
                pe.wait_ge(s_ex, g + 1)
                a, size = (0, DH) if m < H_A else (DH + (m - H_A) // 2 * DV_B, DV_B)

                def transposes(k):
                    bank = free_bank()
                    for j in range(4 * k, min(4 * k + 4, blk[t])):
                        tr = pe.transpose(bank[:, j - 4 * k, :], X[g % 2][:, j * P:(j + 1) * P], idn[:, :])
                    tr.then_inc(s_tr, 1)

                def products(k):
                    n = groups_before(g) + k
                    if g % JOBS == 0:
                        pe.wait_ge(s_v[min(k, 3)], 16)
                        if k == 4:
                            pe.wait_ge(s_v[3], 16)
                    if k == 0 and g > 1:
                        pe.wait_ge(s_out, g - 1)
                    pe.wait_ge(s_pt, n + 1)
                    for j in range(4 * k, min(4 * k + 4, blk[t])):
                        mm = pe.matmul(PV[g % 2][:, 0:size], PTr[n % 3][:, j - 4 * k, :], V[:, j, a:a + size],
                                       start=(j == 0), stop=(j == blk[t] - 1))
                    mm.then_inc(s_pvg, 1)

                early = g + 2 < NG and halves[(g + 2) // JOBS] <= 2 and groups[t] > 1
                transposes(0)
                for k in range(1, groups[t]):
                    transposes(k)
                    if k == 1 and early:
                        queries_keys(g + 2)
                    products(k - 1)
                if g + 2 < NG and not early:
                    queries_keys(g + 2)
                products(groups[t] - 1)

            def finish(t):
                pe.wait_ge(s_fo, t + 1)
                for k in range(2):
                    bank = free_bank()
                    for j in range(4):
                        c = 4 * k + j
                        tr = pe.transpose(bank[:, j, :], O[t % 2][:, c * P:(c + 1) * P], idn[:, :])
                    tr.then_inc(s_ft, 1)

            queries_keys(0)
            queries_keys(1)
            for g in range(NG):
                t = g // JOBS
                if g % JOBS < 2 and t + 1 < PT:
                    scores(t + 1, g % JOBS)
                if g % JOBS == 2 and t > 0:
                    finish(t - 1)
                apply(g)
            finish(PT - 1)

        @block.scalar
        def _(act):
            def relu(t, k):
                n = idx_before(t) + k
                size = min(L, n_of[t] - (k % halves[t]) * L)
                act.wait_ge(s_il, n + 1)
                if n > 1:
                    act.wait_ge(s_ia, n - 1)
                if k == 1 and t > 2:
                    act.wait_ge(s_fs, 16 * (t - 2))
                act.activation(R[n % 2][:, 0:size], LG[:, use_of[("i", n)] % 2, 0:size], ACT.Relu)\
                    .then_inc(s_ir, 1)

            def softmax(g):
                t, m = divmod(g, JOBS)
                slope = (SLOPE_A + [s for s in SLOPE_B for _ in range(2)])[m]
                act.wait_ge(s_nm, g + 1)
                act.activation(X[g % 2][:, 0:n_of[t]], X[g % 2][:, 0:n_of[t]], ACT.Exp,
                               bias=nm[:, g % 2:g % 2 + 1], scale=slope,
                               accum_out=sm[:, g % 2:g % 2 + 1]).then_inc(s_ex, 1)

            def count_signs(t, h):
                n = n_of[t]
                act.wait_ge(s_sel, (t - 1) * SEL + count_step(h))
                act.activation(junk[:, 0:n], S[:, 0:n], ACT.Sign, bias=sv[:, 2:3] if h else 0.0, scale=-1.0,
                               accum_out=sv[:, 3:4]).then_inc(s_sel, 1)

            def take(g, after_two):
                t = g // JOBS
                for k in range(groups[t]):
                    if k == 2:
                        after_two()
                    n = groups_before(g) + k
                    size = min(4, blk[t] - 4 * k)
                    act.wait_ge(s_tr, n + 1)
                    if n >= 3:
                        act.wait_ge(s_pvg, n - 2)
                    act.activation(PTr[n % 3][:, 0:size, :], TP[bank_use[("p", n)] % 2][:, 0:size, :],
                                   ACT.Copy).then_inc(s_pt, 1)

            def finish(t):
                if t > 0:
                    act.wait_ge(s_fs, 16 * t)
                if t + 2 < PT:
                    act.wait_ge(s_ia, idx_before(t + 3))
                for k in range(2):
                    act.wait_ge(s_ft, 2 * t + k + 1)
                    act.activation(OT[:, 4 * k:4 * k + 4, :], TP[bank_use[("f", 2 * t + k)] % 2][:, :, :],
                                   ACT.Copy).then_inc(s_fc, 1)

            act.wait_ge(s_lam, 2)
            act.activation(lv[:, 2:4], lv[:, 0:2], ACT.Exp).then_inc(s_lam, 1)
            softmax(0)
            for g in range(NG):
                t = g // JOBS
                if g % JOBS < 2 and t + 1 < PT:
                    for k in score_halves(t + 1, g % JOBS):
                        relu(t + 1, k)
                if g % JOBS == 2 and t > 0:
                    finish(t - 1)

                def next_softmax():
                    if g + 1 < NG:
                        softmax(g + 1)
                take(g, next_softmax)
                if groups[t] <= 2:
                    next_softmax()
                if t + 1 < PT and counted_by_sign(g % JOBS) is not None:
                    count_signs(t + 1, counted_by_sign(g % JOBS))
            finish(PT - 1)

        @block.vector
        def _(dve):
            dve.wait_ge(s_c, 80)
            dve.memset(X[0][:, :], 0.0).then_inc(s_x0, 1)
            dve.memset(X[1][:, :], 0.0).then_inc(s_x0, 1)
            for i in range(2):
                dve.tensor_tensor_reduce(out=OM[:, i * DH:(i + 1) * DH], in0=lam4[:, 2 * i, :],
                                         in1=lam4[:, 2 * i + 1, :], scale=1.0, scalar=0.0,
                                         op0=ALU.mult, op1=ALU.add, accum_out=lv[:, i:i + 1]).then_inc(s_lam, 1)
            dve.wait_ge(s_lam, 3)
            dve.tensor_tensor(lv[:, 4:5], lv[:, 3:4], lv[:, 2:3], ALU.subtract).then_inc(s_lam, 1)
            dve.wait_ge(s_lam, 4)
            dve.tensor_scalar(lv[:, 5:6], lv[:, 4:5], -LAM_INIT, None, ALU.add).then_inc(s_lam, 1)
            dve.tensor_scalar(gB[:, :], gB[:, :], 1.0 - LAM_INIT, None, ALU.mult).then_inc(s_lam, 1)
            dve.wait_ge(s_lam, 6)
            dve.wait_ge(s_x0, 2)
            dve.wait_ge(s_pow, HALVINGS)

            def add_scores(t, k):
                h, a = k // halves[t], (k % halves[t]) * L
                size = min(L, n_of[t] - a)
                n = idx_before(t) + k
                dve.wait_ge(s_ir, n + 1)
                if h == 0:
                    if k == 0 and t > 1:
                        dve.wait_ge(s_sel, (t - 1) * SEL)
                    ins = dve.tensor_scalar(S[:, a:a + size], R[n % 2][:, 0:size], W[:, t, 0:1], None, ALU.mult)
                else:
                    dve.wait_ge(s_ia, n + 1 - halves[t])
                    ins = dve.scalar_tensor_tensor(S[:, a:a + size], R[n % 2][:, 0:size], W[:, t, h:h + 1],
                                                   S[:, a:a + size], ALU.mult, ALU.add)
                ins.then_inc(s_ia, 1)

            def select(t, k):
                n = n_of[t]
                if k == 0:
                    dve.wait_ge(s_ia, idx_before(t + 1))
                select_step(dve, s_sel, (t - 1) * SEL, k, S[:, 0:n], DA[:, 0:n],
                            DT[:, P * (PT - 1 - t):PKEYS], junk[:, 0:n], sv, powers[:, :],
                            widths[:, :], n, S[0:CHUNK, n - CHUNK:n], by_sign)

            def take(g):
                t, m = divmod(g, JOBS)
                n = n_of[t]
                if g >= 2:
                    dve.wait_ge(s_tr, groups_before(g - 1))
                if m < H_A and t > 0:
                    dve.wait_ge(s_sel, t * SEL)
                i = g % 2
                for k in range(halves[t]):
                    h = halves_before(g) + k
                    a, b = k * L, min(n, k * L + L)
                    D = DA[:, a:b] if m < H_A and t > 0 else DT[:, P * (PT - 1 - t) + a:P * (PT - 1 - t) + b]
                    dve.wait_ge(s_qk, h + 1)
                    if k > 0:
                        dve.wait_ge(s_lx, h)
                    dve.tensor_tensor_reduce(out=X[i][:, a:b], in0=LG[:, use_of[("q", h)] % 2, 0:b - a], in1=D,
                                             scale=1.0, scalar=mx[:, i, k - 1:k] if k else -3.0e38,
                                             op0=ALU.add, op1=ALU.max, accum_out=mx[:, i, k:k + 1])\
                        .then_inc(s_lx, 1)
                slope = (SLOPE_A + [s for s in SLOPE_B for _ in range(2)])[m]
                dve.wait_ge(s_lx, halves_before(g + 1))
                dve.tensor_scalar(nm[:, i:i + 1], mx[:, i, halves[t] - 1:halves[t]], -slope, None, ALU.mult)\
                    .then_inc(s_nm, 1)

            def invert_sum(g):
                i = g % 2
                dve.wait_ge(s_ex, g + 1)
                if g > 0:
                    dve.wait_ge(s_out, g)
                dve.reciprocal(ri[:, i:i + 1], sm[:, i:i + 1]).then_inc(s_ri, 1)

            def times_lambda(g):
                m = g % JOBS
                if m >= H_A and m % 2:
                    dve.wait_ge(s_ri, g + 1)
                    dve.tensor_scalar(rl[:, :], ri[:, g % 2:g % 2 + 1], lv[:, 5:6], None, ALU.mult).then_inc(s_rl, 1)

            def output(g):
                t, m = divmod(g, JOBS)
                i = g % 2
                dve.wait_ge(s_ri, g + 1)
                dve.wait_ge(s_pvg, groups_before(g + 1))
                if m == 0 and t > 1:
                    dve.wait_ge(s_ft, 2 * (t - 1))
                if m < H_A:
                    ins = dve.tensor_scalar(O[t % 2][:, m * DH:(m + 1) * DH], PV[i][:, 0:DH],
                                            ri[:, i:i + 1], None, ALU.mult)
                elif m % 2 == 0:
                    ins = dve.tensor_scalar(OM[:, :], PV[i][:, 0:DV_B], ri[:, i:i + 1], None, ALU.mult)
                else:
                    a = H_A * DH + (m - H_A) // 2 * DV_B
                    dve.wait_ge(s_rl, t * H_B + (m - H_A) // 2 + 1)
                    dve.wait_ge(s_out, g)
                    ins = dve.scalar_tensor_tensor(O[t % 2][:, a:a + DV_B], PV[i][:, 0:DV_B], rl[:, :],
                                                   OM[:, :], ALU.mult, ALU.add)
                ins.then_inc(s_out, 1)

            def finish(t):
                dve.wait_ge(s_out, (t + 1) * JOBS)
                if t > 0:
                    dve.wait_ge(s_fr, t)
                for h in range(H_B):
                    o = O[t % 2][:, H_A * DH + h * DV_B:H_A * DH + (h + 1) * DV_B]
                    if h > 0:
                        dve.wait_ge(s_fq, 4 * t + h)
                    dve.tensor_tensor_reduce(out=OM[:, :], in0=o, in1=o, scale=1.0, scalar=0.0, op0=ALU.mult,
                                             op1=ALU.add, accum_out=fs[:, h:h + 1]).then_inc(s_fq, 1)

            def finish_scale(t):
                dve.wait_ge(s_fr, t + 1)
                for h in range(H_B):
                    o = O[t % 2][:, H_A * DH + h * DV_B:H_A * DH + (h + 1) * DV_B]
                    ins = dve.scalar_tensor_tensor(o, o, fs[:, 4 + h:5 + h], gB[:, :], ALU.mult, ALU.mult)
                ins.then_inc(s_fo, 1)

            def steps(t, first, last):
                return [lambda k=k: select(t, k) for k in range(first, last)]

            take(0)
            for g in range(NG):
                t, m = divmod(g, JOBS)
                before, after = select_steps(m) if t + 1 < PT else ((0, 0), (0, 0))
                early = steps(t + 1, *before)
                if m == JOBS - 1:
                    while early:
                        early.pop(0)()
                if g + 1 < NG:
                    take(g + 1)
                if early:
                    early.pop(0)()
                if g > 0:
                    output(g - 1)
                while early:
                    early.pop(0)()
                if m == 0 and t > 0:
                    finish(t - 1)
                if m < 2 and t + 1 < PT:
                    for k in score_halves(t + 1, m):
                        add_scores(t + 1, k)
                if m == 0 and t > 0:
                    finish_scale(t - 1)
                late = steps(t + 1, *after)
                for step in late[:-1]:
                    step()
                invert_sum(g)
                for step in late[-1:]:
                    step()
                times_lambda(g)
            output(NG - 1)
            finish(PT - 1)
            finish_scale(PT - 1)
    free_semaphores(nc, sems)


def attend_sample(nc, cache_ka, cache_kb, cache_va, cache_vb, kv, qT, wi, dist, slopes, pick, spread, ident, lambdas,
                  sub_g, oA, oB, oT):
    Q = DEC_SEQ
    B = DEC_BATCH
    NB = -(-SKEYS // P)
    XW = NB * P
    GROUPS = -(-NB // 4)
    JOBS = 2 * B
    banks = banks_of(SKEYS)
    ROW = N_META + SEQ

    sems = []
    with ExitStack() as ctx:
        def sb(name, shape, dt=F32):
            return ctx.enter_context(nc.sbuf_tensor("s" + name, shape, dt))

        def sem(name):
            sems.append(nc.alloc_semaphore("s" + name))
            return sems[-1]

        KA = sb("KA", [P, B, SKEYS])
        KB = [sb(f"KB{i}", [P, H_B, SKEYS]) for i in range(2)]
        VA = sb("VA", [P, B, NB, DH])
        VB = [sb(f"VB{i}", [P, NB, H_B * DV_B]) for i in range(2)]
        QS = [VA[:, :, :, :].rearrange("p b j d -> p (b j d)")[:, 0:(H_A + H_I) * 2 * P]
              .rearrange("p (m u q) -> p m u q", u=2, q=P),
              VB[1][:, :, :].rearrange("p j v -> p (j v)")[:, 0:2 * H_B * 2 * P]
              .rearrange("p (m u q) -> p m u q", u=2, q=P)]
        ZK = sb("ZK", [P, KCOLS])
        KN = sb("KN", [P, 5, P])
        QA = sb("QA", [P, B, H_A, Q])
        QI = sb("QI", [P, B, H_I, Q])
        QB = sb("QB", [P, B, H_B, 2 * H_B, Q])
        WI = sb("WI", [H_I * Q, B])
        WS = sb("WS", [H_I * Q, B, P])
        PK = sb("PK", [H_I * Q, Q])
        SPr = sb("SPr", [P, B, P], F32R)
        S = sb("S", [P, SKEYS])
        DA = sb("DA", [P, SKEYS])
        DAr = sb("DAr", [P, SKEYS], F32R)
        DT = sb("DT", [P, SKEYS])
        junk = sb("junk", [P, SKEYS], mybir.dt.uint8)
        X = [sb(f"X{i}", [P, XW]) for i in range(2)]
        PTr = [sb(f"PTr{i}", [P, 4, P]) for i in range(3)]
        OAs = sb("OAs", [P, B, DH])
        OBs = sb("OBs", [P, B, DV_B])
        O = sb("O", [P, D_MODEL])
        SP = O[:, :].rearrange("p (b q) -> p b q", b=B)
        R = [X[i][0:H_I * Q, 0:SKEYS] for i in range(2)]
        OM = X[0][:, 0:2 * H_B * DV_B].rearrange("p (m e) -> p m e", m=2 * H_B)
        OT = X[1][:, 0:D_MODEL].rearrange("p (c q) -> p c q", c=DC)
        gB = sb("gB", [P, DV_B])
        lam4 = sb("lam4", [P, 4, DH])
        lv = sb("lv", [P, 8])
        half = sb("half", [P, 4])
        sv = sb("sv", [P, 8])
        powers = sb("powers", [P, HALVINGS])
        widths = sb("widths", [P, HALVINGS])
        sl = sb("sl", [P, 4])
        mx = sb("mx", [P, 2])
        nm = sb("nm", [P, 2])
        sm = sb("sm", [P, 2])
        ri = sb("ri", [P, 2])
        fs = sb("fs", [P, 8])
        idn = sb("idn", [P, P])
        LG = ctx.enter_context(nc.psum_tensor("sLG", [P, 3 * 512], F32))
        SC = ctx.enter_context(nc.psum_tensor("sSC", [P, 3, 512], F32))
        PV = [ctx.enter_context(nc.psum_tensor(f"sPV{i}", [P, 512], F32)) for i in range(2)]

        s_c = sem("s_c")
        s_z = sem("s_z")
        s_ka = [sem(f"s_ka{b}") for b in range(B)]
        s_kb = [sem(f"s_kb{i}") for i in range(2)]
        s_vb = [sem(f"s_vb{i}") for i in range(2)]
        s_va = sem("s_va")
        s_kt = sem("s_kt")
        s_kn = sem("s_kn")
        s_q = sem("s_q")
        s_ws = sem("s_ws")
        s_kt2 = sem("s_kt2")
        s_kb2 = sem("s_kb2")
        s_lam = sem("s_lam")
        s_half = sem("s_half")
        s_pow = sem("s_pow")
        s_il = sem("s_il")
        s_ir = sem("s_ir")
        s_sc = sem("s_sc")
        s_sb = sem("s_sb")
        s_sel = sem("s_sel")
        s_dr = sem("s_dr")
        s_qk = sem("s_qk")
        s_lx = sem("s_lx")
        s_nm = sem("s_nm")
        s_ex = sem("s_ex")
        s_tr = sem("s_tr")
        s_pt = sem("s_pt")
        s_pvg = sem("s_pvg")
        s_ri = sem("s_ri")
        s_out = sem("s_out")
        s_os = sem("s_os")
        s_ol = sem("s_ol")
        s_of = sem("s_of")
        s_fq = sem("s_fq")
        s_fe = sem("s_fe")
        s_fr = sem("s_fr")
        s_fo = sem("s_fo")
        s_ft = sem("s_ft")
        s_fc = sem("s_fc")
        s_fs = sem("s_fs")

        block = ctx.enter_context(nc.Block())

        @block.sync
        def _(sp):
            for dst, src in ((idn[:, :], ident), (ZK[:, :], kv[ROW:ROW + P, 0:KCOLS]),
                             (QS[0].rearrange("p m u q -> p (m u q)"),
                              qT[PT * P:NT * P, 0:(H_A + H_I) * 2 * P]),
                             (QS[1].rearrange("p m u q -> p (m u q)"),
                              qT[PT * P:NT * P, (H_A + H_I) * 2 * P:]),
                             (PK[:, :], pick), (SP, spread), (DT[:, :], dist), (sl[:, :], slopes),
                             (gB[:, :], sub_g), (lam4[:, :, :], lambdas)):
                sp.dma_start(dst, src).then_inc(s_c, 16)
            for h in range(H_I):
                sp.dma_start(WI[h * Q:(h + 1) * Q, :], wi[PT * P:NT * P, h:h + 1]
                             .rearrange("(b i) o -> i (b o)", b=B), allow_slow_non_contiguous=True).then_inc(s_c, 16)
            for b in range(B):
                sp.dma_start(KA[:, b, 0:PAST], cache_ka[b]).then_inc(s_ka[b], 16)

            def stream(b):
                i = b % 2
                if b >= 2:
                    sp.wait_ge(s_qk, b - 1)
                sp.dma_start(KB[i][:, :, 0:PAST], cache_kb[b]).then_inc(s_kb[i], 16)
                if b == 0:
                    sp.wait_ge(s_z, 5)
                if b >= 2:
                    sp.wait_ge(s_pvg, GROUPS * (b - 1))
                sp.dma_start(VB[i][:, 0:PAST // P, :],
                             cache_vb[b].rearrange("(j p) v -> p j v", p=P)).then_inc(s_vb[i], 16)
                sp.dma_start(VB[i][0:Q, PAST // P, :],
                             kv[ROW + b * Q:ROW + (b + 1) * Q, KCOLS + DH:KV]).then_inc(s_vb[i], 16)
            for b in range(B):
                stream(b)
                if b == 3:
                    for c in range(B):
                        sp.dma_start(VA[:, c, 0:PAST // P, :],
                                     cache_va[c].rearrange("(j p) v -> p j v", p=P)).then_inc(s_va, 16)
                        sp.dma_start(VA[0:Q, c, PAST // P, :],
                                     kv[ROW + c * Q:ROW + (c + 1) * Q, KCOLS:KCOLS + DH]).then_inc(s_va, 16)
            sp.wait_ge(s_out, B)
            for m in range(2 * H_B):
                sp.dma_start(oB[:, m * DV_B:(m + 1) * DV_B].rearrange("(b i) e -> i b e", b=B),
                             OBs[m * Q:(m + 1) * Q, :, :]).then_inc(s_os, 16)
            sp.wait_ge(s_out, 2 * B)
            for h in range(H_A):
                sp.dma_start(oA[:, h * DH:(h + 1) * DH].rearrange("(b i) e -> i b e", b=B),
                             OAs[h * Q:(h + 1) * Q, :, :]).then_inc(s_os, 16)
            sp.wait_ge(s_os, 16 * (2 * H_B + H_A))
            sp.dma_start(O[:, 0:H_A * DH], oA).then_inc(s_ol, 16)
            sp.dma_start(OM.rearrange("p m e -> p (m e)"), oB).then_inc(s_ol, 16)
            sp.wait_ge(s_fc, 2)
            sp.dma_start(oT[:, :, PT * P:NT * P], OT).then_inc(s_fs, 16)
            sp.wait_ge(s_fs, 16)

        @block.gpsimd
        def _(pool):
            pool.memset(half[:, :], -0.5).then_inc(s_half, 1)
            halving_widths(pool, powers, s_pow)
            pool.wait_ge(s_q, 4)
            for t in (VB[0][:, PAST // P, :], VB[1][:, PAST // P, :], VA[:, :, PAST // P, :]):
                pool.memset(t, 0.0).then_inc(s_z, 1)
            pool.wait_ge(s_half, 1)
            pool.wait_ge(s_fq, H_B)
            pool.tensor_scalar(fs[:, 4:8], fs[:, 0:4], 1.0 / DV_B, EPS, ALU.mult, ALU.add).then_inc(s_fe, 1)
            pool.wait_ge(s_fe, 1)
            pool.tensor_tensor(fs[:, 4:8], fs[:, 4:8], half[:, :], ALU.pow).then_inc(s_fr, 1)

        CONST = 16 * (10 + H_I)

        @block.tensor
        def _(pe):
            pe.wait_ge(s_c, CONST)
            for j in range(5):
                tr = pe.transpose(PV[j // 4][:, (j % 4) * P:(j % 4 + 1) * P], ZK[:, j * P:(j + 1) * P], idn[:, :])
                if j in (3, 4):
                    tr.then_inc(s_kt, 1)
            pe.wait_ge(s_q, 4)

            def scores(b):
                pe.wait_ge(s_kt2, b + 1)
                pe.wait_ge(s_ka[b], 16)
                if b > 0:
                    pe.wait_ge(s_ir, b)
                for a, size in banks:
                    mm = pe.matmul(LG[0:H_I * Q, a:a + size],
                                   QI[DH:P, b, :, :].rearrange("p h i -> p (h i)"), KA[DH:P, b, a:a + size],
                                   start=True, stop=True)
                mm.then_inc(s_il, 1)

            def head_sums(b):
                pe.wait_ge(s_ir, b + 1)
                for k, (a, size) in enumerate(banks):
                    mm = pe.matmul(SC[:, k, 0:size], WS[:, b, :], R[b % 2][:, a:a + size],
                                   start=(b == 0), stop=(b == B - 1))
                mm.then_inc(s_sc, 1)

            pe.wait_ge(s_ws, 1 + B)
            scores(0)
            for b in range(B):
                if b + 1 < B:
                    scores(b + 1)
                head_sums(b)

            def logits(g):
                kind, b = divmod(g, B)
                if g > 0:
                    pe.wait_ge(s_lx, g)
                else:
                    pe.wait_ge(s_ir, B)
                if kind == 0:
                    pe.wait_ge(s_kb2, b + 1)
                    for a, size in banks:
                        for h in range(H_B):
                            mm = pe.matmul(LG[:, a:a + size], QB[:, b, h, :, :].rearrange("p m i -> p (m i)"),
                                           KB[b % 2][:, h, a:a + size], start=(h == 0), stop=(h == H_B - 1))
                else:
                    pe.wait_ge(s_dr, 2)
                    for a, size in banks:
                        pe.matmul(LG[:, a:a + size], QA[0:DH, b, :, :].rearrange("p h i -> p (h i)"),
                                  KA[0:DH, b, a:a + size], start=True, stop=False)
                        mm = pe.matmul(LG[:, a:a + size], SPr[:, b, :], DAr[:, a:a + size],
                                       start=False, stop=True)
                mm.then_inc(s_qk, 1)

            def apply(g):
                kind, b = divmod(g, B)
                pe.wait_ge(s_ex, g + 1)

                def transposes(k):
                    n = g * GROUPS + k
                    if n >= 3:
                        pe.wait_ge(s_pt, n - 2)
                    else:
                        pe.wait_ge(s_sb, 1)
                    for j in range(4 * k, min(4 * k + 4, NB)):
                        tr = pe.transpose(SC[:, n % 3, (j % 4) * P:(j % 4 + 1) * P],
                                          X[g % 2][:, j * P:(j + 1) * P], idn[:, :])
                    tr.then_inc(s_tr, 1)

                def products(k):
                    n = g * GROUPS + k
                    if k == 0 and g >= 2:
                        pe.wait_ge(s_out, g - 1)
                    pe.wait_ge(s_pt, n + 1)
                    for j in range(4 * k, min(4 * k + 4, NB)):
                        v = VB[b % 2][:, j, :] if kind == 0 else VA[:, b, j, :]
                        size = H_B * DV_B if kind == 0 else DH
                        mm = pe.matmul(PV[g % 2][:, 0:size], PTr[n % 3][:, j % 4, :], v,
                                       start=(j == 0), stop=(j == NB - 1))
                    mm.then_inc(s_pvg, 1)

                if g == 0:
                    pe.wait_ge(s_kn, 2)
                if kind == 0:
                    pe.wait_ge(s_vb[b % 2], 32 * (b // 2 + 1))
                elif b == 0:
                    pe.wait_ge(s_va, 32 * B)
                transposes(0)
                for k in range(1, GROUPS):
                    transposes(k)
                    products(k - 1)
                products(GROUPS - 1)

            logits(0)
            for g in range(JOBS):
                if g + 1 < JOBS:
                    logits(g + 1)
                apply(g)
            pe.wait_ge(s_fo, 1)
            for k in range(2):
                for j in range(4):
                    c = 4 * k + j
                    tr = pe.transpose(SC[:, k, j * P:(j + 1) * P], O[:, c * P:(c + 1) * P], idn[:, :])
                tr.then_inc(s_ft, 1)

        @block.scalar
        def _(act):
            def softmax(g):
                act.wait_ge(s_nm, g + 1)
                kind = g // B
                act.activation(X[g % 2][:, 0:SKEYS], X[g % 2][:, 0:SKEYS], ACT.Exp,
                               bias=nm[:, g % 2:g % 2 + 1], scale=sl[:, 1 - kind:2 - kind],
                               accum_out=sm[:, g % 2:g % 2 + 1]).then_inc(s_ex, 1)

            def take(g):
                for k in range(GROUPS):
                    n = g * GROUPS + k
                    size = min(4, NB - 4 * k) * P
                    act.wait_ge(s_tr, n + 1)
                    if n >= 3:
                        act.wait_ge(s_pvg, n - 2)
                    act.activation(PTr[n % 3][:, :, :].rearrange("p j q -> p (j q)")[:, 0:size],
                                   SC[:, n % 3, 0:size], ACT.Copy).then_inc(s_pt, 1)

            act.wait_ge(s_lam, 2)
            act.activation(lv[:, 2:4], lv[:, 0:2], ACT.Exp).then_inc(s_lam, 1)
            act.wait_ge(s_kt, 2)
            act.activation(KN[:, 0:4, :].rearrange("p j q -> p (j q)"), PV[0][:, :], ACT.Copy).then_inc(s_kn, 1)
            act.activation(KN[:, 4, :], PV[1][:, 0:P], ACT.Copy).then_inc(s_kn, 1)
            act.wait_ge(s_kn, 2)
            for b in range(B):
                act.activation(KA[:, b, PAST:SKEYS], KN[:, 0, b * Q:(b + 1) * Q], ACT.Copy).then_inc(s_kt2, 1)
            for b in range(B):
                act.wait_ge(s_il, b + 1)
                if b > 1:
                    act.wait_ge(s_sc, b - 1)
                act.activation(R[b % 2], LG[0:H_I * Q, 0:SKEYS], ACT.Relu).then_inc(s_ir, 1)
            act.wait_ge(s_sc, B)
            for k, (a, size) in enumerate(banks):
                ins = act.activation(S[:, a:a + size], SC[:, k, 0:size], ACT.Copy)
            ins.then_inc(s_sb, 1)
            softmax(0)
            for g in range(JOBS):
                take(g)
                if g + 1 < JOBS:
                    softmax(g + 1)
            for k in range(2):
                act.wait_ge(s_ft, k + 1)
                act.activation(OT[:, 4 * k:4 * k + 4, :].rearrange("p j q -> p (j q)"), SC[:, k, :],
                               ACT.Copy).then_inc(s_fc, 1)

        @block.vector
        def _(dve):
            dve.memset(X[0][:, SKEYS:XW], 0.0).then_inc(s_z, 1)
            dve.memset(X[1][:, SKEYS:XW], 0.0).then_inc(s_z, 1)
            dve.memset(QB[:, :, :, :, :], 0.0).then_inc(s_q, 1)
            dve.memset(WS[:, :, :], 0.0).then_inc(s_ws, 1)
            dve.wait_ge(s_c, CONST)
            for i in range(2):
                dve.tensor_tensor_reduce(out=S[:, i * DH:(i + 1) * DH], in0=lam4[:, 2 * i, :],
                                         in1=lam4[:, 2 * i + 1, :], scale=1.0, scalar=0.0,
                                         op0=ALU.mult, op1=ALU.add, accum_out=lv[:, i:i + 1]).then_inc(s_lam, 1)
            (hi, lo), (hiB, loB) = [[q[:, :, u, :].rearrange("p m (b i) -> p b m i", b=B) for u in range(2)]
                                    for q in QS]
            dve.tensor_tensor(QA[0:DH, :, :, :], hi[0:DH, :, 0:H_A, :], lo[0:DH, :, 0:H_A, :], ALU.add)
            dve.tensor_tensor(QI[DH:P, :, :, :], hi[DH:P, :, H_A:H_A + H_I, :],
                              lo[DH:P, :, H_A:H_A + H_I, :], ALU.add).then_inc(s_q, 1)
            dve.wait_ge(s_q, 2)
            for c in range(2):
                for h in range(H_B):
                    m = 2 * h + c
                    ins = dve.tensor_tensor(QB[c * DH:(c + 1) * DH, :, h, 2 * h + c, :],
                                            hiB[c * DH:(c + 1) * DH, :, m, :],
                                            loB[c * DH:(c + 1) * DH, :, m, :], ALU.add)
                ins.then_inc(s_q, 1)
            dve.wait_ge(s_ws, 1)
            for b in range(B):
                dve.tensor_scalar(WS[:, b, b * Q:(b + 1) * Q], PK[:, :], WI[:, b:b + 1], None,
                                  ALU.mult).then_inc(s_ws, 1)
            dve.tensor_copy(SPr[:, :, :], SP).then_inc(s_dr, 1)
            dve.wait_ge(s_lam, 3)
            dve.tensor_tensor(lv[:, 4:5], lv[:, 3:4], lv[:, 2:3], ALU.subtract).then_inc(s_lam, 1)
            dve.wait_ge(s_lam, 4)
            dve.tensor_scalar(lv[:, 5:6], lv[:, 4:5], -LAM_INIT, None, ALU.add).then_inc(s_lam, 1)
            dve.tensor_scalar(gB[:, :], gB[:, :], 1.0 - LAM_INIT, None, ALU.mult).then_inc(s_lam, 1)
            dve.wait_ge(s_z, 5)
            dve.wait_ge(s_kn, 2)

            def keys(b):
                dve.wait_ge(s_kb[b % 2], 16 * (b // 2 + 1))
                if b >= 2:
                    dve.wait_ge(s_qk, b - 1)
                dve.tensor_copy(KB[b % 2][:, :, PAST:SKEYS], KN[:, 1:5, b * Q:(b + 1) * Q]).then_inc(s_kb2, 1)

            def take(g):
                kind = g // B
                i = g % 2
                dve.wait_ge(s_qk, g + 1)
                if g >= 2:
                    dve.wait_ge(s_tr, GROUPS * (g - 1))
                if kind == 0:
                    dve.tensor_tensor_reduce(out=X[i][:, 0:SKEYS], in0=LG[:, 0:SKEYS], in1=DT[:, :], scale=1.0,
                                             scalar=-3.0e38, op0=ALU.add, op1=ALU.max,
                                             accum_out=mx[:, i:i + 1]).then_inc(s_lx, 1)
                else:
                    dve.tensor_scalar(X[i][:, 0:SKEYS], LG[:, 0:SKEYS], 1.0, -3.0e38, ALU.mult, ALU.max,
                                      accum_out=mx[:, i:i + 1]).then_inc(s_lx, 1)
                dve.wait_ge(s_lx, g + 1)
                dve.tensor_scalar(nm[:, i:i + 1], mx[:, i:i + 1], sl[:, 3 - kind:4 - kind], None, ALU.mult)\
                    .then_inc(s_nm, 1)

            def output(g):
                kind, b = divmod(g, B)
                i = g % 2
                dve.wait_ge(s_ex, g + 1)
                dve.reciprocal(ri[:, i:i + 1], sm[:, i:i + 1]).then_inc(s_ri, 1)
                dve.wait_ge(s_ri, g + 1)
                dve.wait_ge(s_pvg, GROUPS * (g + 1))
                if kind == 0:
                    for h in range(H_B):
                        r = slice(32 * h, 32 * h + 32)
                        ins = dve.tensor_scalar(OBs[r, b, :], PV[i][r, h * DV_B:(h + 1) * DV_B],
                                                ri[r, i:i + 1], None, ALU.mult)
                else:
                    ins = dve.tensor_scalar(OAs[:, b, :], PV[i][:, 0:DH], ri[:, i:i + 1], None, ALU.mult)
                ins.then_inc(s_out, 1)

            keys(0)
            take(0)
            dve.wait_ge(s_sb, 1)
            dve.wait_ge(s_pow, HALVINGS)
            SPAN = B - 1
            for g in range(JOBS):
                if g > 0:
                    output(g - 1)
                if g + 1 < B:
                    keys(g + 1)
                if g < SPAN:
                    if g + 1 < JOBS:
                        take(g + 1)
                    for k in range(SEL * g // SPAN, SEL * (g + 1) // SPAN):
                        select_step(dve, s_sel, 0, k, S[:, :], DA[:, :], DT[:, :], junk[:, :], sv,
                                    powers[:, :], widths[:, :], SKEYS)
                    if g == SPAN - 1:
                        dve.wait_ge(s_sel, SEL)
                        dve.tensor_copy(DAr[:, :], DA[:, :]).then_inc(s_dr, 1)
                elif g + 1 < JOBS:
                    take(g + 1)
            output(JOBS - 1)
            dve.wait_ge(s_ol, 32)
            dve.wait_ge(s_lam, 6)
            for h in range(H_B):
                o = O[:, H_A * DH + h * DV_B:H_A * DH + (h + 1) * DV_B]
                dve.scalar_tensor_tensor(o, OM[:, 2 * h + 1, :], lv[:, 5:6], OM[:, 2 * h, :], ALU.mult, ALU.add)\
                    .then_inc(s_of, 1)
            for h in range(H_B):
                o = O[:, H_A * DH + h * DV_B:H_A * DH + (h + 1) * DV_B]
                dve.wait_ge(s_of, H_B)
                dve.tensor_tensor_reduce(out=OM[:, h, :], in0=o, in1=o, scale=1.0, scalar=0.0, op0=ALU.mult,
                                         op1=ALU.add, accum_out=fs[:, h:h + 1]).then_inc(s_fq, 1)
            dve.wait_ge(s_fr, 1)
            for h in range(H_B):
                o = O[:, H_A * DH + h * DV_B:H_A * DH + (h + 1) * DV_B]
                ins = dve.scalar_tensor_tensor(o, o, fs[:, 4 + h:5 + h], gB[:, :], ALU.mult, ALU.mult)
            ins.then_inc(s_fo, 1)
    free_semaphores(nc, sems)


def feed_forward(nc, x, oT, w_o, w_up, w_down, gain, final_g, ident, y):
    F = 512
    FC = F // P
    UPS = D_FF // F
    PIECES = 4 * (1 + UPS)
    LOOPED, NT1, NT2 = 3, 4, 5
    MT = NT2 * P
    DN_OF = 4 + 2 * UPS
    FCS = UPS * FC

    sems = []
    with ExitStack() as ctx:
        def sb(name, shape, dt=F32):
            return ctx.enter_context(nc.sbuf_tensor("f" + name, shape, dt))

        def sem(name):
            sems.append(nc.alloc_semaphore("f" + name))
            return sems[-1]

        W_hi = [sb(f"W_hi{i}", [P, 4096], F32R) for i in range(2)]
        W_lo = [sb(f"W_lo{i}", [P, 4096], F32R) for i in range(2)]
        W_raw = [sb(f"W_raw{i}", [P, 2048]) for i in range(2)]
        A_hi = sb("A_hi", [P, DC, MT], F32R)
        A_lo = sb("A_lo", [P, DC, MT], F32R)
        U_hi = sb("U_hi", [P, FC, MT], F32R)
        U_lo = sb("U_lo", [P, FC, MT], F32R)
        RU = sb("RU", [P, MT])
        U2 = sb("U2", [P, MT])
        H = sb("H", [P, NT2, D_MODEL])
        Y = sb("Y", [P, NT2, D_MODEL])
        TR = [sb(f"TR{i}", [P, DC, P]) for i in range(2)]
        gT = sb("gT", [P, DC])
        gF = sb("gF", [P, D_MODEL])
        idn = sb("idn", [P, P])
        ones = sb("ones", [P, 4])
        const = sb("const", [P, 4])
        ss = sb("ss", [P, 4, NT2])
        UP = [ctx.enter_context(nc.psum_tensor(f"fUP{i}", [P, 2, 512], F32)) for i in range(2)]
        DN = [ctx.enter_context(nc.psum_tensor(f"fDN{i}", [P, 512], F32)) for i in range(4)]

        s_c = sem("s_c")
        s_const = sem("s_const")
        s_w = [sem(f"s_w{i}") for i in range(2)]
        s_whi = sem("s_whi")
        s_wlo = sem("s_wlo")
        s_x = [sem(f"s_x{t}") for t in range(NT2)]
        s_o = [sem(f"s_o{i}") for i in range(2)]
        s_ohi = sem("s_ohi")
        s_olo = sem("s_olo")
        s_dn = sem("s_dn")
        s_dv = sem("s_dv")
        s_sq = sem("s_sq")
        s_y0 = sem("s_y0")
        s_ms = sem("s_ms")
        s_r2 = sem("s_r2")
        s_ahi = sem("s_ahi")
        s_alo = sem("s_alo")
        s_up = sem("s_up")
        s_ru = sem("s_ru")
        s_u2 = sem("s_u2")
        s_uh = sem("s_uh")
        s_ul = sem("s_ul")
        s_t1 = sem("s_t1")
        s_t2 = sem("s_t2")
        s_t3 = sem("s_t3")
        s_t4 = sem("s_t4")
        s_t5 = sem("s_t5")
        s_y = sem("s_y")

        def groups(engine, group):
            with engine.Fori(0, LOOPED, 1) as g:
                group(g, NT1, False)
            group(LOOPED, NT2, True)

        def pairs(engine, pair):
            with engine.Fori(0, UPS - 1, 1) as k:
                pair(k)
            pair(UPS - 1)

        def token(g, t):
            return g * (NT1 * P) + t * P

        ONE = 1

        def dn_base(g):
            return g * (DN_OF * NT1) + ONE

        def w_at(t, h):
            return 2 * h + t if t < 2 else 4 * t - 2 + h

        def t_at(t, nt):
            return 4 * t + 4 if t < nt - 1 else 4 * nt - 2

        def h_whole(t):
            return 4 if t < 2 else 4 * t

        def down_base(g, nt, k):
            return dn_base(g) + 4 * nt + 2 * nt * k

        def quads(nt):
            return [range(a, min(a + 4, 2 * nt)) for a in range(0, 2 * nt, 4)]

        block = ctx.enter_context(nc.Block())

        @block.sync
        def _(sp):
            def w_o_pieces(g):
                for j in range(4):
                    if not (isinstance(g, int) and g == 0 and j < 2):
                        sp.wait_ge(s_wlo, g * PIECES + (j - 1))
                    sp.dma_start(W_raw[j % 2][:, :].rearrange("p (c f) -> p c f", c=4),
                                 w_o[:, 4 * (j % 2):4 * (j % 2) + 4, (j // 2) * 512:(j // 2) * 512 + 512])\
                        .then_inc(s_w[j % 2], 16)

            w_o_pieces(0)

            def group(g, nt, final):
                def pair(k):
                    for j in range(4):
                        sp.wait_ge(s_wlo, g * PIECES + k * 4 + (3 + j))
                        src = w_up[:, 4 * j:4 * j + 4, ds(k * F, F)] if j < 2 else \
                            w_down[:, ds(k * FC + 2 * (j - 2), 2), :]
                        sp.dma_start(W_raw[j % 2][:, :].rearrange("p (c f) -> p c f", c=4 if j < 2 else 2),
                                     src).then_inc(s_w[j % 2], 16)
                pairs(sp, pair)
                if not final:
                    w_o_pieces(g + 1)
            groups(sp, group)

        @block.gpsimd
        def _(pool):
            for i, value in enumerate((1.0 / D_MODEL, EPS, -0.5, 0.0)):
                pool.memset(const[:, i:i + 1], value).then_inc(s_const, 1)
            for i, counted_from_one in enumerate((s_dn, s_dv, s_u2, s_ul)):
                pool.memset(ones[:, i:i + 1], 1.0).then_inc(counted_from_one, 1)
            for dst, src in ((gT[:, :], gain), (gF[:, :], final_g), (idn[:, :], ident)):
                pool.dma_start(dst, src).then_inc(s_c, 16)

            def load_o(g, t):
                if t >= 2 or not (isinstance(g, int) and g == 0):
                    pool.wait_ge(s_olo, g * NT1 + (t - 1 if t >= 2 else 0))
                    pool.wait_ge(s_alo, g * NT1)
                pool.dma_start(TR[t % 2][:, :, :], oT[:, :, ds(token(g, t), P)]).then_inc(s_o[t % 2], 16)

            def load_x(g, t):
                pool.dma_start(H[:, t, :], x[ds(token(g, t) + N_META, P), :]).then_inc(s_x[t], 16)

            for t in range(NT1):
                load_x(0, t)
            for t in range(NT1):
                load_o(0, t)
            pool.wait_ge(s_const, 4)
            zero = const[:, 3:4].to_broadcast([P, D_MODEL])

            def group(g, nt, final):
                if final:
                    load_x(g, nt - 1)
                    load_o(g, nt - 1)
                for t in range(nt):
                    pool.wait_ge(s_sq, g * NT1 + t + 1)
                    pool.tensor_tensor(Y[:, t, :], zero, zero, ALU.add).then_inc(s_y0, 1)
                if not final:
                    for t in range(NT1):
                        load_o(g + 1, t)
                for t in range(nt):
                    pool.wait_ge(s_t2, g * NT1 + t + 1)
                    v = ss[:, 3, t:t + 1]
                    pool.tensor_tensor(v, ss[:, 2, t:t + 1], const[:, 0:1], ALU.mult).then_inc(s_t3, 1)
                    pool.wait_ge(s_t3, g * (2 * NT1) + 2 * t + 1)
                    pool.tensor_tensor(v, v, const[:, 1:2], ALU.add).then_inc(s_t3, 1)
                    pool.wait_ge(s_t3, g * (2 * NT1) + 2 * t + 2)
                    pool.tensor_tensor(v, v, const[:, 2:3], ALU.pow).then_inc(s_t4, 1)
                    pool.wait_ge(s_t5, g * NT1 + t + 1)
                    pool.dma_start(y[ds(token(g, t), P), :], Y[:, t, :]).then_inc(s_y, 16)
                    if not final:
                        load_x(g + 1, t)
            groups(pool, group)
            pool.wait_ge(s_y, 16 * (LOOPED * NT1 + NT2))

        @block.tensor
        def _(pe):
            pe.wait_ge(s_c, 48)

            def three(out, stationary, moving, first, last):
                for i, (a, b) in enumerate(((0, 0), (0, 1), (1, 0))):
                    for o, m in zip(out, moving):
                        mm = pe.matmul(o, stationary[a], m[b], start=first and i == 0, stop=last and i == 2)
                return mm

            def group(g, nt, final):
                base = dn_base(g)
                width = nt * P // (2 if final else 1)
                parts = [slice(i * width, i * width + width) for i in range(nt * P // width)]

                def out_product(t, h):
                    u = w_at(t, h)
                    if u == 0:
                        pe.wait_ge(s_dv, base)
                        pe.wait_ge(s_wlo, g * PIECES + 2)
                    if u == 2:
                        pe.wait_ge(s_wlo, g * PIECES + 4)
                    if u >= 4:
                        pe.wait_ge(s_dv, base + (u - 3))
                    if h == 0:
                        pe.wait_ge(s_olo, g * NT1 + t + 1)
                    tok = slice(t * P, t * P + P)
                    for c in range(DC):
                        col = slice(c * 512, c * 512 + 512)
                        mm = three([DN[u % 4][:, :]], (A_hi[:, c, tok], A_lo[:, c, tok]),
                                   [(W_hi[h][:, col], W_lo[h][:, col])], c == 0, c == DC - 1)
                    mm.then_inc(s_dn, 1)

                def transposes(t):
                    pe.wait_ge(s_dv, base + h_whole(t))
                    for i in range(2):
                        u = t_at(t, nt) + i
                        if u - 3 > h_whole(t):
                            pe.wait_ge(s_dv, base + (u - 3))
                        for q in range(4):
                            c = 4 * i + q
                            tr = pe.transpose(DN[u % 4][:, q * P:q * P + P], H[:, t, c * P:c * P + P], idn[:, :])
                        tr.then_inc(s_dn, 1)

                for t, h in ((0, 0), (1, 0), (0, 1), (1, 1)):
                    out_product(t, h)
                for t in range(nt):
                    transposes(t)
                    if t + 2 < nt:
                        out_product(t + 2, 0)
                        out_product(t + 2, 1)

                def pair(k):
                    pe.wait_ge(s_alo, g * NT1 + nt)
                    pe.wait_ge(s_wlo, g * PIECES + k * 4 + 6)
                    for f in range(FC):
                        if f == 0:
                            pe.wait_ge(s_u2, g * FCS + k * FC + ONE)
                        elif f >= 2:
                            pe.wait_ge(s_u2, g * FCS + k * FC + (f - 1 + ONE))
                        for c in range(DC):
                            col = slice(c * F + f * P, c * F + f * P + P)
                            mm = three([UP[f % 2][:, i, 0:width] for i in range(len(parts))],
                                       (W_hi[0][:, col], W_lo[0][:, col]),
                                       [(A_hi[:, c, s], A_lo[:, c, s]) for s in parts], c == 0, c == DC - 1)
                        mm.then_inc(s_up, 1)
                    pe.wait_ge(s_wlo, g * PIECES + k * 4 + 8)
                    pe.wait_ge(s_dv, down_base(g, nt, k))
                    for quad in quads(nt):
                        for f in range(FC):
                            if quad[0] == 0:
                                pe.wait_ge(s_ul, g * FCS + k * FC + (f + 1 + ONE))
                            for o in quad:
                                t, h = divmod(o, 2)
                                if f == 0 and o >= 4:
                                    pe.wait_ge(s_dv, down_base(g, nt, k) + (o - 3))
                                tok = slice(t * P, t * P + P)
                                col = slice(f * 1024 + h * 512, f * 1024 + h * 512 + 512)
                                mm = three([DN[o % 4][:, :]], (U_hi[:, f, tok], U_lo[:, f, tok]),
                                           [(W_hi[1][:, col], W_lo[1][:, col])], f == 0, f == FC - 1)
                                if f == FC - 1:
                                    mm.then_inc(s_dn, 1)
                pairs(pe, pair)
            groups(pe, group)

        def raw_index(g, slot, j):
            return g * (PIECES // 2) + slot * 2 + (j // 2 + 1)

        @block.scalar
        def _(act):
            def w_hi_part(g, slot, j):
                act.wait_ge(s_w[j % 2], raw_index(g, slot, j) * 16)
                act.activation(W_hi[j // 2][:, (j % 2) * 2048:(j % 2) * 2048 + 2048], W_raw[j % 2][:, :],
                               ACT.Copy).then_inc(s_whi, 1)

            def o_hi_part(g, t):
                tok = slice(t * P, t * P + P)
                act.wait_ge(s_o[t % 2], g * (NT1 * 8) + 16 * (t // 2 + 1))
                act.activation(A_hi[:, :, tok], TR[t % 2][:, :, :], ACT.Copy).then_inc(s_ohi, 1)

            for j in range(4):
                w_hi_part(0, 0, j)
                o_hi_part(0, j)

            def group(g, nt, final):
                base = dn_base(g)
                if final:
                    o_hi_part(g, nt - 1)

                def h_hi_part(t):
                    act.wait_ge(s_dv, base + t_at(t, nt) + 2)
                    act.activation(A_hi[:, :, t * P:t * P + P], TR[t % 2][:, :, :], ACT.Copy).then_inc(s_ahi, 1)

                def h_square(t):
                    act.wait_ge(s_dv, base + h_whole(t))
                    act.activation(Y[:, t, :], H[:, t, :], ACT.Square,
                                   accum_out=ss[:, 0, t:t + 1]).then_inc(s_sq, 1)

                for t in range(nt - 2):
                    h_hi_part(t)
                    h_square(t)
                act.wait_ge(s_dn, base + w_at(nt - 1, 1) + 1)
                w_hi_part(g, 1, 0)
                h_hi_part(nt - 2)
                w_hi_part(g, 1, 1)
                h_hi_part(nt - 1)
                h_square(nt - 2)
                h_square(nt - 1)

                def pair(k):
                    for f in range(FC):
                        width = nt * P // (2 if final else 1)
                        n = nt * P // width
                        act.wait_ge(s_up, g * FCS + k * FC + (f + 1))
                        act.wait_ge(s_u2, g * FCS + k * FC + (f + ONE))
                        act.activation(RU[:, 0:nt * P].rearrange("p (n w) -> p n w", n=n),
                                       UP[f % 2][:, 0:n, 0:width], ACT.Relu).then_inc(s_ru, 1)
                        act.wait_ge(s_u2, g * FCS + k * FC + (f + 1 + ONE))
                        act.activation(U_hi[:, f, 0:nt * P], U2[:, 0:nt * P], ACT.Copy).then_inc(s_uh, 1)
                        if f < 2:
                            act.wait_ge(s_dn, down_base(g, nt, k))
                            w_hi_part(g, k + 1, 2 + f)
                    act.wait_ge(s_up, g * FCS + k * FC + FC)
                    if isinstance(k, int):
                        if not final:
                            w_hi_part(g + 1, 0, 0)
                            w_hi_part(g + 1, 0, 1)
                    else:
                        w_hi_part(g, k + 2, 0)
                        w_hi_part(g, k + 2, 1)
                pairs(act, pair)
                if not final:
                    for t in range(NT1):
                        o_hi_part(g + 1, t)
                    act.wait_ge(s_dn, dn_base(g + 1))
                    w_hi_part(g + 1, 0, 2)
                    w_hi_part(g + 1, 0, 3)
                for t in range(nt):
                    act.wait_ge(s_t1, g * NT1 + t + 1)
                    act.activation(Y[:, t, :], H[:, t, :], ACT.Square,
                                   accum_out=ss[:, 2, t:t + 1]).then_inc(s_t2, 1)
                if not final:
                    act.wait_ge(s_y, g * (NT1 * 16) + NT1 * 16)
            groups(act, group)

        @block.vector
        def _(dve):
            dve.wait_ge(s_c, 48)

            def w_lo_part(g, slot, j):
                col = slice((j % 2) * 2048, (j % 2) * 2048 + 2048)
                dve.wait_ge(s_whi, g * PIECES + slot * 4 + (j + 1))
                dve.tensor_tensor(W_lo[j // 2][:, col], W_raw[j % 2][:, :], W_hi[j // 2][:, col].bitcast(F32),
                                  ALU.subtract).then_inc(s_wlo, 1)

            def a_lo_part(hi_made, count, t, made):
                tok = slice(t * P, t * P + P)
                dve.wait_ge(hi_made, count)
                dve.tensor_tensor(A_lo[:, :, tok], TR[t % 2][:, :, :], A_hi[:, :, tok].bitcast(F32),
                                  ALU.subtract).then_inc(made, 1)

            def o_lo_part(g, t):
                a_lo_part(s_ohi, g * NT1 + t + 1, t, s_olo)

            for j in range(4):
                w_lo_part(0, 0, j)
                o_lo_part(0, j)

            def group(g, nt, final):
                base = dn_base(g)
                if final:
                    o_lo_part(g, nt - 1)

                def add_out(t, h):
                    u = w_at(t, h)
                    cols = slice(h * 512, h * 512 + 512)
                    dve.wait_ge(s_x[t], 16 if t == NT1 else g * 16 + 16)
                    dve.wait_ge(s_dn, base + u + 1)
                    dve.tensor_tensor(H[:, t, cols], DN[u % 4][:, :], H[:, t, cols], ALU.add).then_inc(s_dv, 1)

                def scale_transposed(t):
                    if t < 2:
                        dve.wait_ge(s_olo, g * NT1 + nt)
                    else:
                        dve.wait_ge(s_alo, g * NT1 + (t - 1))
                    for i in range(2):
                        u = t_at(t, nt) + i
                        dve.wait_ge(s_dn, base + u + 1)
                        dve.tensor_tensor(TR[t % 2][:, 4 * i:4 * i + 4, :],
                                          DN[u % 4][:, :].rearrange("p (q c) -> p q c", q=4),
                                          gT[:, 4 * i:4 * i + 4].unsqueeze(2).to_broadcast([P, 4, P]),
                                          ALU.mult).then_inc(s_dv, 1)

                for t, h in ((0, 0), (1, 0), (0, 1), (1, 1)):
                    add_out(t, h)
                for t in range(nt):
                    scale_transposed(t)
                    if t + 2 < nt:
                        add_out(t + 2, 0)
                        add_out(t + 2, 1)
                    else:
                        w_lo_part(g, 1, t + 2 - nt)
                    a_lo_part(s_ahi, g * NT1 + t + 1, t, s_alo)

                def pair(k):
                    for f in range(FC):
                        c = g * FCS + k * FC + f
                        dve.wait_ge(s_ru, c + 1)
                        dve.wait_ge(s_ul, c + ONE)
                        dve.tensor_tensor(U2[:, 0:nt * P], RU[:, 0:nt * P], RU[:, 0:nt * P],
                                          ALU.mult).then_inc(s_u2, 1)
                        dve.wait_ge(s_uh, c + 1)
                        dve.tensor_tensor(U_lo[:, f, 0:nt * P], U2[:, 0:nt * P],
                                          U_hi[:, f, 0:nt * P].bitcast(F32), ALU.subtract).then_inc(s_ul, 1)
                        if f < 2:
                            w_lo_part(g, k + 1, 2 + f)
                    if isinstance(k, int):
                        if not final:
                            w_lo_part(g + 1, 0, 0)
                            w_lo_part(g + 1, 0, 1)
                    else:
                        w_lo_part(g, k + 2, 0)
                        w_lo_part(g, k + 2, 1)
                    for o in range(2 * nt):
                        if isinstance(k, int) and not final and o % 4 == 0:
                            for t in (o // 2, o // 2 + 1):
                                o_lo_part(g + 1, t)
                        t, h = divmod(o, 2)
                        cols = slice(h * 512, h * 512 + 512)
                        dve.wait_ge(s_dn, down_base(g, nt, k) + (o + 1))
                        dve.wait_ge(s_y0, g * NT1 + nt)
                        dve.wait_ge(s_dv, down_base(g, nt, k))
                        dve.tensor_tensor(Y[:, t, cols], DN[o % 4][:, :], Y[:, t, cols], ALU.add)\
                            .then_inc(s_dv, 1)
                pairs(dve, pair)
                if not final:
                    w_lo_part(g + 1, 0, 2)
                    w_lo_part(g + 1, 0, 3)
                dve.tensor_scalar(ss[:, 1, 0:nt], ss[:, 0, 0:nt], 1.0 / D_MODEL, EPS,
                                  ALU.mult, ALU.add).then_inc(s_ms, 1)
                dve.wait_ge(s_ms, g + 1)
                dve.reciprocal(ss[:, 1, 0:nt], ss[:, 1, 0:nt]).then_inc(s_r2, 1)
                dve.wait_ge(s_r2, g + 1)
                dve.wait_ge(s_dv, down_base(g, nt, UPS))

                def output(t):
                    dve.wait_ge(s_t4, g * NT1 + t + 1)
                    dve.scalar_tensor_tensor(Y[:, t, :], H[:, t, :], ss[:, 3, t:t + 1], gF[:, :],
                                             ALU.mult, ALU.mult).then_inc(s_t5, 1)
                for t in range(nt):
                    dve.scalar_tensor_tensor(H[:, t, :], Y[:, t, :], ss[:, 1, t:t + 1], H[:, t, :],
                                             ALU.mult, ALU.add).then_inc(s_t1, 1)
                    if t > 0:
                        output(t - 1)
                output(nt - 1)
            groups(dve, group)
    free_semaphores(nc, sems)


def streaming_step(nc, xT, x, w_keys, w_queries, attn_gain, q_scale, idx_norm, ident, p_dist, s_dist, slopes, pick,
                   spread, lambdas, sub_gain, cache_ka, cache_kb, cache_va, cache_vb, w_o, w_up, w_down, mlp_gain,
                   final_gain, kv, y):
    tokens = NT * P
    kT = nc.dram_tensor("kT", (P, KM, ROWS), F32).ap()
    qT = nc.dram_tensor("qT", (tokens, QM * 2 * P), F32).ap()
    wi = nc.dram_tensor("wi", (tokens, H_I), F32).ap()
    oA = nc.dram_tensor("oA", (P, H_A * DH), F32).ap()
    oB = nc.dram_tensor("oB", (P, 2 * H_B * DV_B), F32).ap()
    oT = nc.dram_tensor("oT", (P, DC, tokens), F32).ap()
    project(nc, True, xT, x, w_keys, attn_gain, ident, None, idx_norm, kv, kT, None)
    project(nc, False, xT, x, w_queries, attn_gain, ident, q_scale, None, None, qT, wi)
    attend_sample(nc, cache_ka, cache_kb, cache_va, cache_vb, kv, qT, wi, s_dist, slopes, pick, spread, ident,
                  lambdas, sub_gain, oA, oB, oT)
    attend_prompt(nc, kT, kv, qT, wi[0:SEQ, :].rearrange("(t p) h -> p t h", p=P), p_dist, ident, lambdas,
                  sub_gain, oT)
    feed_forward(nc, x, oT, w_o, w_up, w_down, mlp_gain, final_gain, ident, y)


def kernel(**inputs):
    import concourse.bacc as bacc
    from concourse.bass_utils import run_bass_kernel_spmd

    def plain(a):
        return np.ascontiguousarray(a)

    def rows_to_partitions(a):
        return plain(a.reshape(-1, P, a.shape[-1]).transpose(1, 0, 2))

    def every_partition(a):
        return plain(np.broadcast_to(a, (P,) + a.shape))

    given = {name: np.asarray(a) for name, a in inputs.items()}
    x = np.concatenate([given["meta_tokens"], given["x_prompt"][0], given["x_sample"].reshape(P, D_MODEL)])
    widths = (H_A * DH, DH, DH, H_I * DH, DH, H_I, 2 * H_B * DH, 2 * H_B * DH, H_B * DV_B)
    qa, ka, va, qi, ki, wi, qb, kb, vb = np.split(given["w_in"][0], np.cumsum(widths)[:-1], axis=1)

    scale = np.concatenate([np.repeat([DH ** -0.5 / s for s in SLOPE_A], DH), np.full(H_I * DH, DH ** -0.5),
                            np.repeat([DH ** -0.5 / s for s in SLOPE_B], 2 * DH),
                            np.full(H_I, H_I ** -0.5)]).astype(np.float32)
    row = np.arange(P)
    key = np.arange(PKEYS)[None]
    last = SEQ - P + N_META
    p_dist = -np.abs(last + row[:, None] - key).astype(np.float32)
    p_dist[(row[:, None] < CHUNK) & (key >= last + CHUNK)] = -BIG
    s_dist = -np.abs(PAST + row[:, None] % DEC_SEQ - np.arange(SKEYS)[None]).astype(np.float32)
    slope_a = np.array(SLOPE_A)[row // DEC_SEQ]
    slope_b = np.array(SLOPE_B)[row // (2 * DEC_SEQ)]
    slopes = np.stack([slope_a, slope_b, -slope_a, -slope_b], 1).astype(np.float32)
    pick = (np.arange(H_I * DEC_SEQ)[:, None] % DEC_SEQ == np.arange(DEC_SEQ)[None]).astype(np.float32)
    spread = ((row[:, None, None] // DEC_SEQ == np.arange(DEC_BATCH)[None, :, None])
              & (row[:, None, None] % DEC_SEQ == row[None, None, :] % DEC_SEQ)).astype(np.float32)

    arrays = {
        "xT": rows_to_partitions(x.T), "x": x,
        "w_keys": rows_to_partitions(np.concatenate([ka, ki, kb, va, vb], 1)),
        "w_queries": rows_to_partitions(np.concatenate([qa, qi, qb, wi], 1)),
        "attn_gain": plain(given["attn_norm_g"][0].reshape(DC, P).T), "q_scale": every_partition(scale),
        "idx_norm": every_partition(np.stack([given["idx_k_norm_g"][0], given["idx_k_norm_b"][0]])),
        "ident": np.eye(P, dtype=np.float32), "p_dist": p_dist, "s_dist": s_dist, "slopes": slopes,
        "pick": pick, "spread": spread,
        "lambdas": every_partition(np.stack([given[n][0] for n in
                                             ("lambda_q1", "lambda_k1", "lambda_q2", "lambda_k2")])),
        "sub_gain": every_partition(given["subln_g"][0]),
        "cache_ka": plain(np.concatenate([given["cache_a_k"][0], given["cache_a_idx_k"][0]], 2).transpose(0, 2, 1)),
        "cache_kb": plain(given["cache_b_k"][0].transpose(0, 3, 4, 2, 1).reshape(DEC_BATCH, P, H_B, PAST)),
        "cache_va": plain(given["cache_a_v"][0]),
        "cache_vb": plain(given["cache_b_v"][0].reshape(DEC_BATCH, PAST, H_B * DV_B)),
        "w_o": rows_to_partitions(given["w_o"][0]), "w_up": rows_to_partitions(given["w_up"][0]),
        "w_down": rows_to_partitions(given["w_down"][0]),
        "mlp_gain": plain(given["mlp_norm_g"][0].reshape(DC, P).T),
        "final_gain": every_partition(given["final_norm_g"]),
    }
    nc = bacc.Bacc("TRN2", target_bir_lowering=False, num_devices=1)
    args = [nc.dram_tensor(name, a.shape, mybir.dt.from_np(a.dtype), kind="ExternalInput").ap()
            for name, a in arrays.items()]
    kv_out = nc.dram_tensor("kv", (ROWS, KV), F32, kind="ExternalOutput").ap()
    y_out = nc.dram_tensor("y", (NT * P, D_MODEL), F32, kind="ExternalOutput").ap()
    streaming_step(nc, *args, kv_out, y_out)
    result = run_bass_kernel_spmd(nc, [arrays], core_ids=[0]).results[0]

    y, kv = result["y"], result["kv"]
    new_ka, new_ki, new_kb, new_va, new_vb = np.split(kv, [DH, 2 * DH, KCOLS, KCOLS + DH], axis=1)

    def of_prompt(a, *shape):
        return a[:PKEYS].reshape((1, 1, PKEYS) + shape)

    def of_sample(a, *shape):
        return a[PKEYS:].reshape((1, DEC_BATCH, DEC_SEQ) + shape)

    caches = tuple(part(a, *shape) for part in (of_prompt, of_sample)
                   for a, shape in ((new_ka, (DH,)), (new_va, (DH,)), (new_ki, (DH,)),
                                    (new_kb, (H_B, 2, DH)), (new_vb, (H_B, DV_B))))
    return (y[:SEQ].reshape(1, SEQ, D_MODEL), y[SEQ:].reshape(DEC_BATCH, DEC_SEQ, D_MODEL)) + caches
```
